# Optimizing a Trainium2 kernel written in Bass

```python
import math
import jax, jax.numpy as jnp
from jax import lax
import numpy as np

D_MODEL = 1024
BATCH = 1
SEQ = 256
DEPTH = 2

D_MIX = D_MODEL
ATT_HEADS = 8
ATT_HD = 64
D_ATT = ATT_HEADS * ATT_HD
D_CONV = 256
CONV_GROUPS = 4
CONV_K = 31
D_RNN = 256
RNN_BLOCKS = 4
RNN_BD = D_RNN // RNN_BLOCKS
RNN_CONV_K = 4
RG_C = 8.0
Q_BLOCK = 128
EPS = 1e-6

Q0, Q1 = 0, D_ATT
K0, K1 = Q1, Q1 + D_ATT
V0, V1 = K1, K1 + D_ATT
F0, F1 = V1, V1 + ATT_HEADS
C0, C1 = F1, F1 + 2 * D_CONV
R0, R1 = C1, C1 + D_RNN
G0, G1 = R1, R1 + D_RNN
N_IN = G1

PEER_HEADS = 8
N_KEYS = 128
N_EXPERTS = N_KEYS * N_KEYS
D_KEY = 256
D_HALF = D_KEY // 2
TOPK = 16
TOK_CHUNK = 128


def rms_norm(x, g):
    xf = x.astype(jnp.float32)
    y = xf * lax.rsqrt(jnp.mean(xf * xf, axis=-1, keepdims=True) + EPS)
    return (y * g.astype(jnp.float32)).astype(x.dtype)

def layer_norm(x, g, b):
    xf = x.astype(jnp.float32)
    mu = jnp.mean(xf, axis=-1, keepdims=True)
    var = jnp.mean(jnp.square(xf - mu), axis=-1, keepdims=True)
    y = (xf - mu) * lax.rsqrt(var + EPS)
    return (y * g.astype(jnp.float32) + b.astype(jnp.float32)).astype(x.dtype)

def causal_dwconv(x, w, b):
    k = w.shape[0]
    y = lax.conv_general_dilated(
        x, w[:, None, :], window_strides=(1,), padding=[(k - 1, 0)],
        dimension_numbers=("NWC", "WIO", "NWC"), feature_group_count=x.shape[-1])
    return y + b

def forgetting_attention(q, k, v, log_f):
    b, s, h, hd = q.shape
    nb = s // Q_BLOCK
    scale = 1.0 / math.sqrt(hd)
    cum = jnp.cumsum(log_f.astype(jnp.float32), axis=1).transpose(0, 2, 1)
    q = q.transpose(0, 2, 1, 3)
    k = k.transpose(0, 2, 1, 3)
    v = v.transpose(0, 2, 1, 3)
    qb = q.reshape(b, h, nb, Q_BLOCK, hd).transpose(2, 0, 1, 3, 4)
    cb = cum.reshape(b, h, nb, Q_BLOCK).transpose(2, 0, 1, 3)
    kpos = jnp.arange(s)

    def one_block(args):
        qi, ci, blk = args
        qpos = blk * Q_BLOCK + jnp.arange(Q_BLOCK)
        logits = jnp.einsum("bhqd,bhkd->bhqk", qi, k).astype(jnp.float32) * scale
        logits = logits + ci[..., :, None] - cum[:, :, None, :]
        logits = jnp.where(kpos[None, :] <= qpos[:, None], logits, -jnp.inf)
        p = jax.nn.softmax(logits, axis=-1)
        return jnp.einsum("bhqk,bhkd->bhqd", p.astype(v.dtype), v)

    o = lax.map(one_block, (qb, cb, jnp.arange(nb)))
    return o.transpose(1, 0, 3, 2, 4).reshape(b, s, h * hd)

def conformer_conv(u, w_dw, b_dw, ln_g, ln_b):
    a, gate = u[..., :D_CONV], u[..., D_CONV:]
    y = a * jax.nn.sigmoid(gate)
    y = causal_dwconv(y, w_dw, b_dw)
    y = layer_norm(y, ln_g, ln_b)
    return jax.nn.silu(y)

def _lin_combine(c1, c2):
    a1, b1 = c1
    a2, b2 = c2
    return a1 * a2, a2 * b1 + b2

def rglru_block(xr, gate_in, conv_w, conv_b, w_r, b_r, w_i, b_i, lam):
    xr = causal_dwconv(xr, conv_w, conv_b)
    b, s, c = xr.shape
    xh = xr.reshape(b, s, RNN_BLOCKS, RNN_BD)
    r = jax.nn.sigmoid(jnp.einsum("bshi,hij->bshj", xh, w_r).reshape(b, s, c) + b_r)
    i = jax.nn.sigmoid(jnp.einsum("bshi,hij->bshj", xh, w_i).reshape(b, s, c) + b_i)
    log_a = -RG_C * r.astype(jnp.float32) * jax.nn.softplus(-lam.astype(jnp.float32))
    a = jnp.exp(log_a)
    mult = jnp.sqrt(-jnp.expm1(2.0 * log_a))
    bterm = mult * (i * xr).astype(jnp.float32)
    _, hs = lax.associative_scan(_lin_combine, (a, bterm), axis=1)
    return hs.astype(xr.dtype) * jax.nn.gelu(gate_in)

def peer(xn, wq, k1, k2, u_tab, v_tab):
    b, s, d = xn.shape
    t = b * s
    xt = xn.reshape(t, d)
    q = (xt @ wq).reshape(t, PEER_HEADS, D_KEY)
    q1, q2 = q[..., :D_HALF], q[..., D_HALF:]
    s1 = jnp.einsum("thd,hnd->thn", q1, k1).astype(jnp.float32)
    s2 = jnp.einsum("thd,hnd->thn", q2, k2).astype(jnp.float32)
    v1, i1 = lax.top_k(s1, TOPK)
    v2, i2 = lax.top_k(s2, TOPK)
    cand = (v1[..., :, None] + v2[..., None, :]).reshape(t, PEER_HEADS, TOPK * TOPK)
    sv, ci = lax.top_k(cand, TOPK)
    e1 = jnp.take_along_axis(i1, ci // TOPK, axis=-1)
    e2 = jnp.take_along_axis(i2, ci % TOPK, axis=-1)
    nc = t // TOK_CHUNK
    experts = (e1 * N_KEYS + e2).reshape(nc, TOK_CHUNK, PEER_HEADS * TOPK)
    gates = jax.nn.softmax(sv, axis=-1).astype(xn.dtype).reshape(nc, TOK_CHUNK, PEER_HEADS * TOPK)
    xc = xt.reshape(nc, TOK_CHUNK, d)

    def chunk(args):
        xi, ei, gi = args
        hid = jax.nn.gelu(jnp.einsum("td,tkd->tk", xi, u_tab[ei]))
        return jnp.einsum("tk,tkd->td", gi * hid, v_tab[ei])

    out = lax.map(chunk, (xc, experts, gates))
    return out.reshape(b, s, d)

def first_inputs(seed: int = 0) -> dict:
    key = jax.random.key(seed)
    ks = jax.random.split(key, 26)
    L, D = DEPTH, D_MODEL
    nrm = jax.random.normal
    u_lr = jax.random.uniform(ks[14], (L, D_RNN), minval=0.9, maxval=0.999)
    p_lr = u_lr ** (1.0 / RG_C)
    lam = jnp.log(p_lr) - jnp.log1p(-p_lr)
    return {
        "x": nrm(ks[0], (BATCH, SEQ, D), jnp.float32),
        "norm1_g": 1.0 + 0.01 * nrm(ks[1], (L, D)),
        "w_in": nrm(ks[2], (L, D, N_IN)) * D ** -0.5,
        "b_forget": jax.random.uniform(ks[3], (L, ATT_HEADS), minval=1.0, maxval=5.0),
        "conv_dw_w": nrm(ks[4], (L, CONV_K, D_CONV)) * CONV_K ** -0.5,
        "conv_dw_b": 0.01 * nrm(ks[5], (L, D_CONV)),
        "conv_ln_g": 1.0 + 0.01 * nrm(ks[6], (L, D_CONV)),
        "conv_ln_b": 0.01 * nrm(ks[7], (L, D_CONV)),
        "rg_conv_w": nrm(ks[8], (L, RNN_CONV_K, D_RNN)) * RNN_CONV_K ** -0.5,
        "rg_conv_b": 0.01 * nrm(ks[9], (L, D_RNN)),
        "rg_w_r": nrm(ks[10], (L, RNN_BLOCKS, RNN_BD, RNN_BD)) * RNN_BD ** -0.5,
        "rg_b_r": 0.01 * nrm(ks[11], (L, D_RNN)),
        "rg_w_i": nrm(ks[12], (L, RNN_BLOCKS, RNN_BD, RNN_BD)) * RNN_BD ** -0.5,
        "rg_b_i": 0.01 * nrm(ks[13], (L, D_RNN)),
        "rg_lambda": lam,
        "w_out": nrm(ks[15], (L, D_MIX, D)) * D_MIX ** -0.5,
        "norm2_g": 1.0 + 0.01 * nrm(ks[16], (L, D)),
        "peer_wq": nrm(ks[17], (L, D, PEER_HEADS * D_KEY)) * D ** -0.5,
        "peer_k1": nrm(ks[18], (L, PEER_HEADS, N_KEYS, D_HALF)) * D_HALF ** -0.5,
        "peer_k2": nrm(ks[19], (L, PEER_HEADS, N_KEYS, D_HALF)) * D_HALF ** -0.5,
        "peer_u": nrm(ks[20], (L, N_EXPERTS, D)) * D ** -0.5,
        "peer_v": nrm(ks[21], (L, N_EXPERTS, D)) * 0.5 * PEER_HEADS ** -0.5,
        "final_g": 1.0 + 0.01 * nrm(ks[22], (D,)),
    }

def first_block(x, norm1_g, w_in, b_forget, conv_dw_w, conv_dw_b, conv_ln_g, conv_ln_b,
              rg_conv_w, rg_conv_b, rg_w_r, rg_b_r, rg_w_i, rg_b_i, rg_lambda, w_out,
              norm2_g, peer_wq, peer_k1, peer_k2, peer_u, peer_v, final_g):
    b, s, _ = x.shape
    for l in range(DEPTH):
        h = rms_norm(x, norm1_g[l])
        proj = h @ w_in[l]
        q = proj[..., Q0:Q1].reshape(b, s, ATT_HEADS, ATT_HD)
        k = proj[..., K0:K1].reshape(b, s, ATT_HEADS, ATT_HD)
        v = proj[..., V0:V1].reshape(b, s, ATT_HEADS, ATT_HD)
        log_f = jax.nn.log_sigmoid((proj[..., F0:F1] + b_forget[l]).astype(jnp.float32))
        y_att = forgetting_attention(q, k, v, log_f)
        y_conv = conformer_conv(proj[..., C0:C1], conv_dw_w[l], conv_dw_b[l],
                                conv_ln_g[l], conv_ln_b[l])
        y_rnn = rglru_block(proj[..., R0:R1], proj[..., G0:G1], rg_conv_w[l], rg_conv_b[l],
                            rg_w_r[l], rg_b_r[l], rg_w_i[l], rg_b_i[l], rg_lambda[l])
        mixed = jnp.concatenate([y_att, y_conv.astype(x.dtype), y_rnn.astype(x.dtype)], axis=-1)
        x = x + mixed @ w_out[l]
        h2 = rms_norm(x, norm2_g[l])
        x = x + peer(h2, peer_wq[l], peer_k1[l], peer_k2[l], peer_u[l], peer_v[l])
    return rms_norm(x, final_g)


GRID_W = 64
CTX_LEN = 256
N_EVEN = (DEPTH + 1) // 2
N_ODD = DEPTH // 2
MIX_WIDTH = D_MODEL
DA_HEADS = 4
DA_DK = 64
DA_DV = 2 * DA_DK
MLA_HEADS = 4
MLA_NOPE = 128
MLA_ROPE = 64
MLA_V = 128
MLA_Q_LORA = 256
MLA_KV_LORA = 128
EV_IN = 3 * DA_HEADS * 2 * DA_DK + MLA_Q_LORA + MLA_KV_LORA + MLA_ROPE
NA_HEADS = 16
NA_DH = 64
NA_KH = 8
NA_KW = 16
D_FF = -(-8 * D_MODEL // (3 * 256)) * 256
ROPE_THETA = 10000.0
NEG_INF = -1e30


def rms_norm_2(x, g):
    xf = x.astype(jnp.float32)
    y = xf * lax.rsqrt(jnp.mean(xf * xf, axis=-1, keepdims=True) + EPS)
    return (y * g.astype(jnp.float32)).astype(x.dtype)

def softmax_f32(s):
    return jax.nn.softmax(s.astype(jnp.float32), axis=-1)

def adaln(cond, mod_w, mod_b):
    return jnp.split(jax.nn.silu(cond) @ mod_w + mod_b, 6, axis=-1)

def modulate(h, shift, scale):
    return h * (1 + scale) + shift

def swiglu(h, w_in, w_out):
    g, u = jnp.split(h @ w_in, 2, axis=-1)
    return (jax.nn.silu(g) * u) @ w_out

def axial_rope_tables(S, dim):
    t = jnp.arange(S)
    row = (t // GRID_W).astype(jnp.float32)
    col = (t % GRID_W).astype(jnp.float32)
    half = dim // 2
    inv = ROPE_THETA ** (-jnp.arange(0, half, 2, dtype=jnp.float32) / half)
    ar = row[:, None] * inv
    ac = col[:, None] * inv
    return (jnp.cos(ar), jnp.sin(ar), jnp.cos(ac), jnp.sin(ac))

def _rotate(x, cos, sin):
    x1, x2 = jnp.split(x, 2, axis=-1)
    return jnp.concatenate([x1 * cos - x2 * sin, x1 * sin + x2 * cos], axis=-1)

def apply_axial_rope(x, tables):
    cr, sr, cc, sc = tables
    xr, xc = jnp.split(x, 2, axis=-1)
    return jnp.concatenate([_rotate(xr, cr, sr), _rotate(xc, cc, sc)], axis=-1).astype(x.dtype)

def sweep_query_blocks(fn, *qs):
    S = qs[0].shape[-2]
    nb = S // Q_BLOCK
    blocks = tuple(jnp.moveaxis(q.reshape(q.shape[:-2] + (nb, Q_BLOCK, q.shape[-1])), -3, 0) for q in qs)
    out = lax.map(lambda a: fn(*a), blocks)
    out = jnp.moveaxis(out, 0, -3)
    return out.reshape(out.shape[:-3] + (S, out.shape[-1]))

def merge_heads(*outs):
    return jnp.concatenate([o.transpose(0, 2, 1, 3).reshape(o.shape[0], o.shape[2], -1) for o in outs], axis=-1)

def even_project(h, w_in, da_q_g, da_k_g, mla_q_a_g, mla_w_uq, mla_kv_a_g, mla_w_ukv, mla_q_g, mla_k_g, mla_kr_g):
    B, T, _ = h.shape
    n_dq = DA_HEADS * 2 * DA_DK
    idx = [n_dq, 2 * n_dq, 3 * n_dq, 3 * n_dq + MLA_Q_LORA, 3 * n_dq + MLA_Q_LORA + MLA_KV_LORA]
    dq, dk, dv, cq, ckv, kr = jnp.split(h @ w_in, idx, axis=-1)
    dq = rms_norm_2(dq.reshape(B, T, DA_HEADS, 2, DA_DK), da_q_g).transpose(0, 2, 3, 1, 4)
    dk = rms_norm_2(dk.reshape(B, T, DA_HEADS, 2, DA_DK), da_k_g).transpose(0, 2, 3, 1, 4)
    dv = dv.reshape(B, T, DA_HEADS, DA_DV).transpose(0, 2, 1, 3)
    q = (rms_norm_2(cq, mla_q_a_g) @ mla_w_uq).reshape(B, T, MLA_HEADS, MLA_NOPE + MLA_ROPE)
    q = rms_norm_2(q, mla_q_g).transpose(0, 2, 1, 3)
    qn, qr = q[..., :MLA_NOPE], q[..., MLA_NOPE:]
    kv = (rms_norm_2(ckv, mla_kv_a_g) @ mla_w_ukv).reshape(B, T, MLA_HEADS, MLA_NOPE + MLA_V)
    kn = rms_norm_2(kv[..., :MLA_NOPE], mla_k_g).transpose(0, 2, 1, 3)
    mv = kv[..., MLA_NOPE:].transpose(0, 2, 1, 3)
    kr = rms_norm_2(kr, mla_kr_g)
    return dq, dk, dv, qn, qr, kn, kr, mv

def diff_attend(q, k, v, lam, lam_init, out_g):
    s = jnp.einsum('bhiqd,bhikd->bhiqk', q, k) * (DA_DK ** -0.5)
    p = softmax_f32(s)
    a = p[:, :, 0] - lam * p[:, :, 1]
    o = jnp.einsum('bhqk,bhkd->bhqd', a.astype(v.dtype), v)
    return rms_norm_2(o, out_g) * (1.0 - lam_init)

def mla_attend(qn, qr, kn, kr, v):
    s = (jnp.einsum('bhqd,bhkd->bhqk', qn, kn) + jnp.einsum('bhqd,bkd->bhqk', qr, kr)) * ((MLA_NOPE + MLA_ROPE) ** -0.5)
    p = softmax_f32(s)
    return jnp.einsum('bhqk,bhkd->bhqd', p.astype(v.dtype), v)

def even_mixer(hx, hc, need_ctx, w_in, da_q_g, da_k_g, lam, lam_init, da_out_g,
               mla_q_a_g, mla_w_uq, mla_kv_a_g, mla_w_ukv, mla_q_g, mla_k_g, mla_kr_g):
    proj = lambda h: even_project(h, w_in, da_q_g, da_k_g, mla_q_a_g, mla_w_uq, mla_kv_a_g, mla_w_ukv,
                                  mla_q_g, mla_k_g, mla_kr_g)
    dq_x, dk_x, dv_x, qn_x, qr_x, kn_x, kr_x, mv_x = proj(hx)
    dq_c, dk_c, dv_c, qn_c, qr_c, kn_c, kr_c, mv_c = proj(hc)
    S = hx.shape[1]
    tab_da = axial_rope_tables(S, DA_DK)
    tab_mla = axial_rope_tables(S, MLA_ROPE)
    dq_x = apply_axial_rope(dq_x, tab_da)
    dk_x = apply_axial_rope(dk_x, tab_da)
    qr_x = apply_axial_rope(qr_x, tab_mla)
    kr_x = apply_axial_rope(kr_x, tab_mla)
    dk_all = jnp.concatenate([dk_c, dk_x], axis=-2)
    dv_all = jnp.concatenate([dv_c, dv_x], axis=-2)
    kn_all = jnp.concatenate([kn_c, kn_x], axis=-2)
    kr_all = jnp.concatenate([kr_c, kr_x], axis=-2)
    mv_all = jnp.concatenate([mv_c, mv_x], axis=-2)
    da_x = sweep_query_blocks(lambda q: diff_attend(q, dk_all, dv_all, lam, lam_init, da_out_g), dq_x)
    mla_x = sweep_query_blocks(lambda a, b: mla_attend(a, b, kn_all, kr_all, mv_all), qn_x, qr_x)
    y_x = merge_heads(da_x, mla_x)
    y_c = None
    if need_ctx:
        da_c = diff_attend(dq_c, dk_c, dv_c, lam, lam_init, da_out_g)
        mla_c = mla_attend(qn_c, qr_c, kn_c, kr_c, mv_c)
        y_c = merge_heads(da_c, mla_c)
    return y_x, y_c

def odd_project(h, w_in, q_g, k_g):
    B, T, _ = h.shape
    q, k, v = jnp.split((h @ w_in).reshape(B, T, 3 * NA_HEADS, NA_DH), 3, axis=2)
    q = rms_norm_2(q, q_g).transpose(0, 2, 1, 3)
    k = rms_norm_2(k, k_g).transpose(0, 2, 1, 3)
    return q, k, v.transpose(0, 2, 1, 3)

def dense_attend(q, k, v):
    p = softmax_f32(jnp.einsum('bhqd,bhkd->bhqk', q, k) * (NA_DH ** -0.5))
    return jnp.einsum('bhqk,bhkd->bhqd', p.astype(v.dtype), v)

def na_latent(q, k, v, kc, vc, rpb):
    B, H, S, d = q.shape
    rows = S // GRID_W
    kh = min(NA_KH, rows)
    kg = k.reshape(B, H, rows, GRID_W, d)
    vg = v.reshape(B, H, rows, GRID_W, d)
    qg = q.reshape(B, H, rows, GRID_W, d)
    cols = jnp.arange(GRID_W)
    col_start = jnp.clip(cols - NA_KW // 2, 0, GRID_W - NA_KW)
    col_valid = (cols[None, :] >= col_start[:, None]) & (cols[None, :] < col_start[:, None] + NA_KW)
    dc_idx = jnp.clip(cols[None, :] - cols[:, None], -(NA_KW - 1), NA_KW - 1) + NA_KW - 1
    rpb_c = rpb[:, :, dc_idx]
    scale = NA_DH ** -0.5

    def row_step(args):
        r, q_row = args
        rs = jnp.clip(r - kh // 2, 0, rows - kh)
        kb = lax.dynamic_slice_in_dim(kg, rs, kh, axis=2)
        vb = lax.dynamic_slice_in_dim(vg, rs, kh, axis=2)
        dr_idx = rs + jnp.arange(kh) - r + NA_KH - 1
        bias = jnp.take(rpb_c, dr_idx, axis=1).transpose(0, 2, 1, 3)
        s_loc = jnp.einsum('bhqd,bhiwd->bhqiw', q_row, kb).astype(jnp.float32) * scale + bias
        s_loc = jnp.where(col_valid[:, None, :], s_loc, NEG_INF).reshape(B, H, GRID_W, kh * GRID_W)
        s_ctx = jnp.einsum('bhqd,bhkd->bhqk', q_row, kc).astype(jnp.float32) * scale
        p = softmax_f32(jnp.concatenate([s_loc, s_ctx], axis=-1))
        p_loc = p[..., :kh * GRID_W].reshape(B, H, GRID_W, kh, GRID_W).astype(v.dtype)
        p_ctx = p[..., kh * GRID_W:].astype(v.dtype)
        return jnp.einsum('bhqiw,bhiwd->bhqd', p_loc, vb) + jnp.einsum('bhqk,bhkd->bhqd', p_ctx, vc)

    out = lax.map(row_step, (jnp.arange(rows), jnp.moveaxis(qg, 2, 0)))
    return jnp.moveaxis(out, 0, 2).reshape(B, H, S, d)

def odd_mixer(hx, hc, need_ctx, w_in, q_g, k_g, rpb):
    q_x, k_x, v_x = odd_project(hx, w_in, q_g, k_g)
    q_c, k_c, v_c = odd_project(hc, w_in, q_g, k_g)
    y_x = merge_heads(na_latent(q_x, k_x, v_x, k_c, v_c, rpb))
    y_c = merge_heads(dense_attend(q_c, k_c, v_c)) if need_ctx else None
    return y_x, y_c

def second_inputs(seed: int = 0) -> dict:
    key = jax.random.key(seed)
    ks = iter(jax.random.split(key, 40))
    nrm = lambda shape, s: jax.random.normal(next(ks), shape, jnp.float32) * s
    gain = lambda shape: 1.0 + 0.1 * jax.random.normal(next(ks), shape, jnp.float32)
    D = D_MODEL
    return {
        "x": nrm((BATCH, SEQ, D), 1.0),
        "c": nrm((BATCH, D), 1.0),
        "ctx": nrm((BATCH, CTX_LEN, D), 1.0),
        "c_ctx": nrm((D,), 1.0),
        "mod_w": nrm((DEPTH, D, 6 * D), 0.5 * D ** -0.5),
        "mod_b": nrm((DEPTH, 6 * D), 0.02),
        "norm_mix_g": gain((DEPTH, D)),
        "norm_ffn_g": gain((DEPTH, D)),
        "w_out": nrm((DEPTH, MIX_WIDTH, D), MIX_WIDTH ** -0.5),
        "ffn_w_in": nrm((DEPTH, D, 2 * D_FF), D ** -0.5),
        "ffn_w_out": nrm((DEPTH, D_FF, D), D_FF ** -0.5),
        "ev_w_in": nrm((N_EVEN, D, EV_IN), D ** -0.5),
        "da_q_g": gain((N_EVEN, DA_DK)),
        "da_k_g": gain((N_EVEN, DA_DK)),
        "da_lq1": nrm((N_EVEN, DA_DK), 0.1),
        "da_lk1": nrm((N_EVEN, DA_DK), 0.1),
        "da_lq2": nrm((N_EVEN, DA_DK), 0.1),
        "da_lk2": nrm((N_EVEN, DA_DK), 0.1),
        "da_out_g": gain((N_EVEN, DA_DV)),
        "mla_q_a_g": gain((N_EVEN, MLA_Q_LORA)),
        "mla_w_uq": nrm((N_EVEN, MLA_Q_LORA, MLA_HEADS * (MLA_NOPE + MLA_ROPE)), MLA_Q_LORA ** -0.5),
        "mla_kv_a_g": gain((N_EVEN, MLA_KV_LORA)),
        "mla_w_ukv": nrm((N_EVEN, MLA_KV_LORA, MLA_HEADS * (MLA_NOPE + MLA_V)), MLA_KV_LORA ** -0.5),
        "mla_q_g": gain((N_EVEN, MLA_NOPE + MLA_ROPE)),
        "mla_k_g": gain((N_EVEN, MLA_NOPE)),
        "mla_kr_g": gain((N_EVEN, MLA_ROPE)),
        "od_w_in": nrm((N_ODD, D, 3 * NA_HEADS * NA_DH), D ** -0.5),
        "na_q_g": gain((N_ODD, NA_DH)),
        "na_k_g": gain((N_ODD, NA_DH)),
        "na_rpb": nrm((N_ODD, NA_HEADS, 2 * NA_KH - 1, 2 * NA_KW - 1), 0.5),
    }

def second_block(x, c, ctx, c_ctx, mod_w, mod_b, norm_mix_g, norm_ffn_g, w_out, ffn_w_in, ffn_w_out,
              ev_w_in, da_q_g, da_k_g, da_lq1, da_lk1, da_lq2, da_lk2, da_out_g,
              mla_q_a_g, mla_w_uq, mla_kv_a_g, mla_w_ukv, mla_q_g, mla_k_g, mla_kr_g,
              od_w_in, na_q_g, na_k_g, na_rpb):
    for l in range(DEPTH):
        need_ctx = l < DEPTH - 1
        sh_a, sc_a, g_a, sh_f, sc_f, g_f = [m[:, None, :] for m in adaln(c, mod_w[l], mod_b[l])]
        csh_a, csc_a, cg_a, csh_f, csc_f, cg_f = adaln(c_ctx, mod_w[l], mod_b[l])
        hx = modulate(rms_norm_2(x, norm_mix_g[l]), sh_a, sc_a)
        hc = modulate(rms_norm_2(ctx, norm_mix_g[l]), csh_a, csc_a)
        e = l // 2
        if l % 2 == 0:
            lam_init = 0.8 - 0.6 * math.exp(-0.3 * l)
            lam = (jnp.exp(jnp.sum(da_lq1[e] * da_lk1[e]).astype(jnp.float32))
                   - jnp.exp(jnp.sum(da_lq2[e] * da_lk2[e]).astype(jnp.float32)) + lam_init)
            y_x, y_c = even_mixer(hx, hc, need_ctx, ev_w_in[e], da_q_g[e], da_k_g[e], lam, lam_init, da_out_g[e],
                                  mla_q_a_g[e], mla_w_uq[e], mla_kv_a_g[e], mla_w_ukv[e],
                                  mla_q_g[e], mla_k_g[e], mla_kr_g[e])
        else:
            y_x, y_c = odd_mixer(hx, hc, need_ctx, od_w_in[e], na_q_g[e], na_k_g[e], na_rpb[e])
        x = x + g_a * (y_x @ w_out[l])
        x = x + g_f * swiglu(modulate(rms_norm_2(x, norm_ffn_g[l]), sh_f, sc_f), ffn_w_in[l], ffn_w_out[l])
        if need_ctx:
            ctx = ctx + cg_a * (y_c @ w_out[l])
            ctx = ctx + cg_f * swiglu(modulate(rms_norm_2(ctx, norm_ffn_g[l]), csh_f, csc_f), ffn_w_in[l], ffn_w_out[l])
    return x


def setup_inputs(seed=0):
    out = dict(first_inputs(seed))
    for name, value in second_inputs(seed + 1).items():
        if name != "x":
            out[name + "_2"] = value
    return out


def reference(
    x, norm1_g, w_in, b_forget, conv_dw_w, conv_dw_b, conv_ln_g, conv_ln_b, rg_conv_w,
    rg_conv_b, rg_w_r, rg_b_r, rg_w_i, rg_b_i, rg_lambda, w_out, norm2_g, peer_wq, peer_k1,
    peer_k2, peer_u, peer_v, final_g, c_2, ctx_2, c_ctx_2, mod_w_2, mod_b_2, norm_mix_g_2,
    norm_ffn_g_2, w_out_2, ffn_w_in_2, ffn_w_out_2, ev_w_in_2, da_q_g_2, da_k_g_2, da_lq1_2,
    da_lk1_2, da_lq2_2, da_lk2_2, da_out_g_2, mla_q_a_g_2, mla_w_uq_2, mla_kv_a_g_2,
    mla_w_ukv_2, mla_q_g_2, mla_k_g_2, mla_kr_g_2, od_w_in_2, na_q_g_2, na_k_g_2, na_rpb_2,
):
    x = first_block(
        x, norm1_g, w_in, b_forget, conv_dw_w, conv_dw_b, conv_ln_g, conv_ln_b, rg_conv_w,
        rg_conv_b, rg_w_r, rg_b_r, rg_w_i, rg_b_i, rg_lambda, w_out, norm2_g, peer_wq, peer_k1,
        peer_k2, peer_u, peer_v, final_g,
    )
    return second_block(
        x, c_2, ctx_2, c_ctx_2, mod_w_2, mod_b_2, norm_mix_g_2, norm_ffn_g_2, w_out_2,
        ffn_w_in_2, ffn_w_out_2, ev_w_in_2, da_q_g_2, da_k_g_2, da_lq1_2, da_lk1_2, da_lq2_2,
        da_lk2_2, da_out_g_2, mla_q_a_g_2, mla_w_uq_2, mla_kv_a_g_2, mla_w_ukv_2, mla_q_g_2,
        mla_k_g_2, mla_kr_g_2, od_w_in_2, na_q_g_2, na_k_g_2, na_rpb_2,
    )


_drawn_inputs = setup_inputs


def setup_inputs(seed=0):
    import zlib

    import numpy as np

    out = dict(_drawn_inputs(seed))
    spreads = {}
    factors = {'norm1_g': 4.226,
     'conv_dw_b': 3.557,
     'conv_ln_g': 5.264,
     'conv_ln_b': 5.631,
     'rg_b_r': 8.0,
     'rg_b_i': 8.0,
     'norm2_g': 4.131,
     'final_g': 5.522,
     'norm_mix_g_2': 3.751,
     'da_q_g_2': 7.094,
     'da_k_g_2': 8.0,
     'da_lq1_2': 64.0,
     'da_lk1_2': 64.0,
     'da_lq2_2': 8.0,
     'da_lk2_2': 8.0,
     'da_out_g_2': 3.143,
     'mla_q_a_g_2': 8.0,
     'mla_kv_a_g_2': 8.0,
     'mla_q_g_2': 8.0,
     'mla_k_g_2': 8.0,
     'mla_kr_g_2': 8.0,
     'na_q_g_2': 8.0,
     'na_k_g_2': 8.0,
     'na_rpb_2': 7.107}
    for name, (base, spread) in spreads.items():
        noise = np.random.default_rng([zlib.crc32(name.encode()), seed]).standard_normal(out[name].shape)
        drawn = base * np.exp(spread * noise) if base else spread * noise
        out[name] = __import__('jax').numpy.asarray(drawn.astype(out[name].dtype))
    for name, factor in factors.items():
        out[name] = (out[name] * factor).astype(out[name].dtype)
    return out
```

```python
import math
from contextlib import ExitStack

import numpy as np
import concourse.bass as bass
from concourse import mybir

F32 = mybir.dt.float32
U32 = mybir.dt.uint32
ALU = mybir.AluOpType
ACT = mybir.ActivationFunctionType
AXX = mybir.AxisListType.X

P = 128
D = 1024
C = D // P
T = 256
T2 = 2 * T
L = 2
HEADS, HD = 8, 64
TAPS, RTAPS = 31, 4
PH, TOPK, NKEY = 8, 16, 128
NQ = 4
EQ = NKEY // NQ
BT = T // EQ
R = 8
FF = 2816
KF = FF // P
NEG = -1e30
EPS = 1e-6
LAM_INIT = 0.2

N_IN, N_OUT, N_WQ = 20, 8, 16
N_PEER = 2 * NKEY
N1 = N_IN + N_OUT + N_WQ + N_PEER
PHASES = [("u", 0, None), ("u", 1, 0), ("v", 0, None), ("u", 2, 1), ("v", 1, None),
          ("u", 3, 2), ("v", 2, 3), ("v", 3, None)]
N_MOD = 48
N_FIN, N_FOUT = 2 * KF, KF
PROJ = [16, 24]
MOD0 = L * N1
SB = [MOD0, MOD0 + N_MOD + PROJ[0] + N_OUT + N_FIN + N_FOUT]
NTILES = SB[1] + N_MOD + PROJ[1] + N_OUT + N_FIN + N_FOUT

CONST = {}
_at = 0
for _name, _w in ([(f"{n}{l}", w) for l in range(L) for n, w in (
        ("g1_", C), ("g2_", C), ("bf", 1), ("cw", 2 * TAPS), ("cb", 2), ("lg", 2), ("lb", 2),
        ("rw", 2 * RTAPS), ("rb", 2), ("wr", 2 * P), ("wi", 2 * P), ("br", 2), ("bi", 2), ("lam", 2),
        ("wf", C * HEADS), ("mb", N_MOD), ("gm", C), ("gf", C))] +
        [("gfin", C), ("cc", 2 * C), ("daq", 1), ("dak", 1), ("lq", 2), ("lk", 2), ("dao", 1),
         ("mqa", 2), ("mkva", 1), ("mqn", 1), ("mqr", 1), ("mk", 1), ("mkr", 1), ("naq", 1), ("nak", 1),
         ("ident", P), ("ones", P), ("half", P), ("rot", P),
         ("mask", P), ("iota", P), ("cos", T), ("sin", T)]):
    CONST[_name] = (_at, _w)
    _at += _w
NCONST = _at


def cols(a):
    return np.ascontiguousarray(np.asarray(a).reshape(-1, P).T)


def tiles(w):
    k, n = w.shape
    return w.reshape(k // P, P, n // P, P).transpose(2, 1, 0, 3).reshape(n // P, P, k)


def weight_stream(i):
    out = []
    for l in range(L):
        w = i["w_in"][l]
        c0 = 3 * 512 + HEADS
        feat = np.concatenate([w[:, c0:c0 + 512], w[:, c0 + 512:c0 + 768], w[:, c0 + 768:c0 + 1024],
                               w[:, 0:512], w[:, 512:1024], w[:, 1024:1536]], 1)
        out += [tiles(feat), tiles(i["w_out"][l]), tiles(i["peer_wq"][l])]
        u = i["peer_u"][l].reshape(NKEY, NKEY, C, P).transpose(1, 3, 2, 0).reshape(NKEY, P, C * NKEY)
        v = i["peer_v"][l].reshape(NKEY, NKEY, D).transpose(1, 0, 2)
        for kind, q, _ in PHASES:
            out.append((u if kind == "u" else v)[q * EQ:(q + 1) * EQ])
    for l in range(L):
        out.append(tiles(i["mod_w_2"][l]))
        if l == 0:
            w = i["ev_w_in_2"][0]
            kr = np.pad(w[:, 1920:1984], ((0, 0), (0, 64)))
            out.append(tiles(np.concatenate([w[:, 0:1024], w[:, 1536:1920], kr, w[:, 1024:1536]], 1)))
        else:
            out.append(tiles(i["od_w_in_2"][0]))
        out.append(tiles(i["w_out_2"][l]))
        f = i["ffn_w_in_2"][l].reshape(D, 2, KF, P).transpose(0, 2, 1, 3).reshape(D, 2 * FF)
        out.append(tiles(f))
        f = i["ffn_w_out_2"][l].reshape(KF // 2, 2, P, 2, 4, P).transpose(3, 0, 2, 1, 4, 5)
        out.append(f.reshape(KF, P, D))
    return np.ascontiguousarray(np.concatenate(out, 0))


def constants(i):
    c = np.zeros((P, NCONST), np.float32)

    def put(name, a):
        at, w = CONST[name]
        a = np.asarray(a)
        c[:a.shape[0], at:at + w] = a

    def twice(a):
        return np.concatenate([a, a])[:, None]

    for l in range(L):
        put(f"g1_{l}", cols(i["norm1_g"][l]))
        put(f"g2_{l}", cols(i["norm2_g"][l]))
        put(f"bf{l}", i["b_forget"][l][:, None])
        put(f"cw{l}", i["conv_dw_w"][l].reshape(TAPS, 2, P).transpose(2, 1, 0).reshape(P, 2 * TAPS))
        put(f"cb{l}", cols(i["conv_dw_b"][l]))
        put(f"lg{l}", cols(i["conv_ln_g"][l]))
        put(f"lb{l}", cols(i["conv_ln_b"][l]))
        put(f"rw{l}", i["rg_conv_w"][l].reshape(RTAPS, 2, P).transpose(2, 1, 0).reshape(P, 2 * RTAPS))
        put(f"rb{l}", cols(i["rg_conv_b"][l]))
        for n, k in (("wr", "rg_w_r"), ("wi", "rg_w_i")):
            w = np.zeros((P, 2, P), np.float32)
            for c_ in range(2):
                for b in range(2):
                    w[64 * b:64 * b + 64, c_, 64 * b:64 * b + 64] = i[k][l][2 * c_ + b]
            put(f"{n}{l}", w.reshape(P, 2 * P))
        put(f"br{l}", cols(i["rg_b_r"][l]))
        put(f"bi{l}", cols(i["rg_b_i"][l]))
        put(f"lam{l}", cols(i["rg_lambda"][l]))
        put(f"wf{l}", i["w_in"][l][:, 1536:1544].reshape(C, P, HEADS).transpose(1, 0, 2).reshape(P, -1))
        put(f"mb{l}", cols(i["mod_b_2"][l]))
        put(f"gm{l}", cols(i["norm_mix_g_2"][l]))
        put(f"gf{l}", cols(i["norm_ffn_g_2"][l]))
    put("gfin", cols(i["final_g"]))
    put("cc", np.stack([cols(i["c_ctx_2"]), cols(i["c_2"][0])], 2).reshape(P, 2 * C))
    put("daq", twice(i["da_q_g_2"][0]))
    put("dak", twice(i["da_k_g_2"][0]))
    put("lq", np.stack([i["da_lq1_2"][0], i["da_lq2_2"][0]], 1))
    put("lk", np.stack([i["da_lk1_2"][0], i["da_lk2_2"][0]], 1))
    put("dao", i["da_out_g_2"][0][:, None])
    put("mqa", cols(i["mla_q_a_g_2"][0]))
    put("mkva", cols(i["mla_kv_a_g_2"][0]))
    put("mqn", i["mla_q_g_2"][0][:128, None])
    put("mqr", i["mla_q_g_2"][0][128:, None])
    put("mk", i["mla_k_g_2"][0][:, None])
    put("mkr", i["mla_kr_g_2"][0][:, None])
    put("naq", twice(i["na_q_g_2"][0]))
    put("nak", twice(i["na_k_g_2"][0]))
    p = np.arange(P)
    put("ident", np.eye(P))
    put("ones", np.ones((P, P)))
    put("half", (p[:, None] // 64 == p[None, :] // 64))
    rot = np.zeros((P, P))
    for m in range(P):
        rot[m + 16 if m % 32 < 16 else m - 16, m] = -1.0 if m % 32 < 16 else 1.0
    put("rot", rot)
    put("mask", np.where(p[None, :] <= p[:, None], 0.0, NEG))
    put("iota", np.tile(p[None, :], (P, 1)))
    t = np.arange(T)
    half = 32
    inv = (np.float32(10000.0) ** (-np.arange(0, half, 2, dtype=np.float32) / np.float32(half))).astype(np.float32)
    d = p % 64
    pos = np.where(d[:, None] < 32, (t // 64)[None, :], (t % 64)[None, :]).astype(np.float32)
    ang = (pos * inv[d % 16][:, None]).astype(np.float32)
    put("cos", np.cos(ang).astype(np.float32))
    put("sin", np.sin(ang).astype(np.float32))
    return c


def mla_blocks(i):
    uq = i["mla_w_uq_2"][0].reshape(2, P, 4, 192)
    uq = np.pad(uq, ((0, 0), (0, 0), (0, 0), (0, 64))).reshape(2, P, 4, 2, P)
    out = [uq[c, :, h, part] for h in range(4) for part in range(2) for c in range(2)]
    ukv = i["mla_w_ukv_2"][0].reshape(P, 4, 256)
    out += [ukv[:, h, :128] for h in range(4)] + [ukv[:, h, 128:] for h in range(4)]
    return np.ascontiguousarray(np.stack(out, 1).reshape(P, 24 * 128))


def key_blocks(i):
    k = np.stack([i["peer_k1"], i["peer_k2"]], 2)
    return np.ascontiguousarray(k.transpose(0, 4, 1, 2, 3).reshape(L, P, 2 * PH * NKEY))


def na_bias(i):
    q, k = np.arange(T), np.arange(T)
    dr = (k // 64)[None, :] - (q // 64)[:, None]
    dc = (k % 64)[None, :] - (q % 64)[:, None]
    start = np.clip(q % 64 - 8, 0, 48)
    ok = ((k % 64)[None, :] >= start[:, None]) & ((k % 64)[None, :] < start[:, None] + 16)
    b = i["na_rpb_2"][0][:, dr + 7, np.clip(dc, -15, 15) + 15]
    b = np.where(ok[None], b, np.float32(NEG)).astype(np.float32)
    return np.ascontiguousarray(b.reshape(16, 2, P, T).transpose(0, 2, 1, 3).reshape(16, P, 2 * T))


def after(eng, sem, value):
    if not isinstance(value, int) or value > 0:
        eng.wait_ge(sem, value)


def steps(eng, n, peel, body):
    if peel:
        body(0)
    with eng.Fori(1 if peel else 0, n) as it:
        body(it)


def build(nc, wts, cst_d, keys_d, mla_d, bias_d, x_d, ctx_d, out_d, stop_after=None):
    ctx = ExitStack()
    with ctx:
        def sb(name, shape, dt=F32):
            return ctx.enter_context(nc.sbuf_tensor(name, shape, dt))

        sems = {}

        def S(name):
            if name not in sems:
                sems[name] = ctx.enter_context(nc.semaphore(name))
            return sems[name]

        X = sb("X", [P, C, T2])
        H = sb("H", [P, C, T2])
        ring = sb("ring", [P, R, 8, P])
        K = sb("K", [P, NCONST])
        NAR = 33408
        arena = sb("arena", [P, NAR])
        eps = sb("eps", [P, 1])
        zero = sb("zero", [P, P])
        nlam = sb("nlam", [P, 1])
        col = sb("col", [P, 96])
        bank = [ctx.enter_context(nc.psum_tensor(f"bank{i}", [P, 512], F32)) for i in range(8)]

        XS = slice(T, T2)

        def k(name, a=0, b=None):
            at, w = CONST[name]
            return K[:, at + a:at + (w if b is None else b)]

        top = [0]

        def area(*dims, at=None):
            n = int(np.prod(dims))
            o = top[0] if at is None else at
            top[0] = o + n
            assert o + n <= NAR, (o, n)
            a = arena[:, o:o + n]
            if len(dims) == 2:
                a = a.rearrange("p (a b) -> p a b", a=dims[0])
            if len(dims) == 3:
                a = a.rearrange("p (a b c) -> p a b c", a=dims[0], b=dims[1])
            return a

        GH = [area(EQ, T, at=0), area(EQ, T, at=EQ * T)]
        top[0] = 0
        cvA, cvG, yconv, cen, sqc = (area(2, T) for _ in range(5))
        ypad, rpad = area(2, T + TAPS - 1), area(2, T + RTAPS - 1)
        gateG, xr, rg, ig, la, aa, th, m2, bx, hs = (area(2, T) for _ in range(10))
        qT, kT = area(4, T), area(4, T)
        vtok = area(2, 512)
        fz = [area(T) for _ in range(6)]
        cum, ncum = area(T), area(T)
        sel = area(HEADS, P)
        top[0] = 16384
        mixT = area(C, T)
        hi0 = top[0]
        sq = area(C, T2)
        rt, rs = area(T2), area(T2)
        biasT = area(HEADS, 3 * P, at=hi0 + 5120)
        sc = [area(3 * P) for _ in range(2)]
        Pm = [area(3 * P) for _ in range(2)]
        PT = [area(3 * P) for _ in range(2)]
        cT = area(2, HEADS)
        top[0] = 16384
        keysT = area(16, P)
        assert top[0] <= hi0
        top[0] = hi0 + 5120
        qs = [area(T) for _ in range(2)]
        w1 = area(P)
        v12, i12, if12 = area(2, 16, 16), area(2, 16, 16), area(2, 16, 16)
        cand, cand2 = area(256), area(256)
        sv, ci = area(2, 8, 16), area(2, 8, 16)
        ca, cb = area(2, 8, 16), area(2, 8, 16)
        gte = area(2, 3, P)
        ssum = area(2, 8)
        gT = area(3, T)
        oneh = area(8, 16, 16)
        top[0] -= 2 * BT * P
        Aoh = [area(BT, P) for _ in range(2)]
        Boh, Bg = [area(BT, EQ) for _ in range(2)], [area(BT, EQ) for _ in range(2)]
        i12u, ciu = i12.bitcast(U32), ci.bitcast(U32)
        cau, cbu = ca.bitcast(U32), cb.bitcast(U32)

        raw, vda = area(12, T2, at=0), area(4, 512)
        raw2, vml = area(12, T2), area(4, 512)
        sqg = [area(2, T2) for _ in range(2)]
        assert top[0] <= hi0
        mlaw = area(24, P, at=hi0 + 5120)
        grt = [area(T2) for _ in range(4)]
        grs = [area(T2) for _ in range(2)]
        Pb = [area(2, T2) for _ in range(2)]
        AT = [area(4, P) for _ in range(2)]
        modv = [area(N_MOD, 2) for _ in range(L)]
        gA, gF = area(C, 2), area(C, 2)
        csil, csig = area(C, 2), area(C, 2)
        mix2 = sq
        rtmp = [area(T, at=hi0 - 2048 + i * T) for i in range(2)]
        hid, sg = area(KF, T2, at=0), [area(T2) for _ in range(2)]
        qN, kN, vN = area(C, T, at=0), area(C, T2), area(4, D)
        NB = 4
        nab = [area(2, T) for _ in range(NB)]
        assert top[0] <= hi0 - 2048
        G_MLA, G_DA, G_NA = 11, 19, 23

        OUT_RES = 4 * C
        NORMS = ["n1.0", "n2.0", "n1.1", "n2.1", "fin", "a0", "f0", "a1", "f1"]
        ident = k("ident")
        rope_tiles = [raw[:, i, :] for i in (0, 1, 2, 3, 4, 5, 6, 7, 11)] + [raw2[:, 2 * h + 1, :] for h in range(4)]
        block = ctx.enter_context(nc.Block())

        def slot_value(i, it=0):
            return 16 * (i // R + 1) + 16 * it

        @block.sync
        def _(sp):
            sp.dma_start(K[:], cst_d).then_inc(S("const_in"), 16)
            sp.dma_start(X[:, :, 0:T], ctx_d.rearrange("(c p) t -> p c t", p=P)).then_inc(S("ctx_in"), 16)
            sp.dma_start(X[:, :, XS], x_d.rearrange("(c p) t -> p c t", p=P)).then_inc(S("x_in"), 16)

            def load(i, slot):
                sp.dma_start(ring[:, slot].rearrange("p a b -> p (a b)"),
                             wts[bass.ds(i, 1), :, :].rearrange("o p n -> (o p) n")).then_inc(S(f"tile{slot}"), 16)

            total = NTILES if stop_after is None else stop_after
            for s in range(R):
                load(s, s)
            with sp.Fori(1, total // R) as it:
                for s in range(R):
                    sp.wait_ge(S("tile_done"), it * R + (s - R + 1))
                    load(it * R + s, s)
            for i in range(total // R * R, total):
                sp.wait_ge(S("tile_done"), i - R + 1)
                load(i, i % R)
            sp.wait_ge(S("res_ev"), OUT_RES)
            sp.dma_start(out_d.rearrange("(c p) t -> p c t", p=P), X[:, :, XS]).then_inc(S("out"), 16)
            sp.wait_ge(S("out"), 16)

        @block.tensor
        def _(pe):
            def mm(out, lhsT, rhs, first, last):
                return nc.tensor.matmul(out, lhsT, rhs, start=first, stop=last)

            def tile_ready(i, it=0):
                pe.wait_ge(S(f"tile{i % R}"), slot_value(i, it))
                return ring[:, i % R]

            def norm_sums(name, n=T):
                j = NORMS.index(name)
                pe.wait_ge(S("norm_sq"), j + 1)
                for c in range(C):
                    m = mm(bank[7][:, 0:n], k("ones"), sq[:, c, 0:n], c == 0, c == C - 1)
                m.then_inc(S("norm_ss"), 1)

            def feature_tile(i, out, rhs, it=0):
                w = tile_ready(i, it)
                for c in range(C):
                    m = mm(out, w[:, c, :], rhs[:, c, :], c == 0, c == C - 1)
                m.then_inc(S("tile_done"), 1)

            Hx = H[:, :, XS]
            pe.wait_ge(S("const_in"), 16)
            for l in range(L):
                t0 = l * N1
                norm_sums(f"n1.{l}")
                pe.wait_ge(S("norm_out"), NORMS.index(f"n1.{l}") + 1)
                for c in range(C):
                    m = mm(bank[4][0:HEADS, 0:T], k(f"wf{l}", c * HEADS, (c + 1) * HEADS), Hx[:, c, :], c == 0, c == C - 1)
                m.then_inc(S("f_mm"), 1)
                for m_ in range(16):
                    if m_ >= 4:
                        pe.wait_ge(S("proj_ev"), N_IN * l + m_ - 3)
                    feature_tile(t0 + m_, bank[m_ % 4][:, 0:T], Hx)
                    if m_ == 11:
                        pe.wait_ge(S("xr_ready"), l + 1)
                        for g, wname in ((0, "wr"), (1, "wi")):
                            for c in range(2):
                                m = mm(bank[5 + g][:, c * T:(c + 1) * T], k(f"{wname}{l}", c * P, (c + 1) * P),
                                       xr[:, c, :], True, True)
                        m.then_inc(S("rg_mm"), 1)
                for n in range(4):
                    pe.wait_ge(S("proj_ev"), N_IN * l + 16 + n - 3)
                    w = tile_ready(t0 + 16 + n)
                    for tt in range(2):
                        for c in range(C):
                            m = mm(bank[n][:, tt * P:(tt + 1) * P], H[:, c, T + tt * P:T + (tt + 1) * P],
                                   w[:, c, :], c == 0, c == C - 1)
                    m.then_inc(S("tile_done"), 1)
                pe.wait_ge(S("cum_ready"), l + 1)
                pe.wait_ge(S("proj_ev"), N_IN * (l + 1))
                pe.wait_ge(S("rg_ev"), 2 * l + 2)
                for tt in range(2):
                    mm(bank[5][:, tt * HEADS:(tt + 1) * HEADS], cum[0:HEADS, tt * P:(tt + 1) * P],
                       ident[0:HEADS, 0:HEADS], True, True)
                for h in range(HEADS):
                    m = mm(bank[(0, 1, 2, 4)[h // 2]][:, (h % 2) * T:(h % 2 + 1) * T], sel[0:HEADS, h, :],
                           ncum[0:HEADS, :], True, True)
                m.then_inc(S("bc_mm"), 1)
                pe.wait_ge(S("bc_ev"), l + 1)
                for h in range(HEADS + 1):
                    if h < HEADS:
                        po, hc, b = slice(64 * (h % 2), 64 * (h % 2) + 64), h // 2, bank[4 + h % 2]
                        if h >= 2:
                            pe.wait_ge(S("att_sc"), HEADS * l + h - 1)
                        mm(b[:, 0:P], qT[po, hc, 0:P], kT[po, hc, 0:P], True, True)
                        mm(b[:, P:3 * P], qT[po, hc, P:T], kT[po, hc, :], True, True).then_inc(S("att_mm"), 1)
                    if h >= 1:
                        g = h - 1
                        po, hc = slice(64 * (g % 2), 64 * (g % 2) + 64), g // 2
                        pe.wait_ge(S("p_ready"), HEADS * l + g + 1)
                        if g >= 2:
                            pe.wait_ge(S("pt_ev"), HEADS * l + g - 1)
                        for i in range(3):
                            m = nc.tensor.transpose(bank[6 + g % 2][:, i * P:(i + 1) * P], Pm[g % 2][:, i * P:(i + 1) * P], ident)
                        m.then_inc(S("pt_mm"), 1)
                        pe.wait_ge(S("pt_ev"), HEADS * l + g + 1)
                        if hc >= 2:
                            pe.wait_ge(S("y_ev"), 4 * l + hc - 1)
                        yb = bank[hc % 2]
                        mm(yb[po, 0:T], vtok[:, 0, g * HD:(g + 1) * HD], PT[g % 2][:, 0:T], True, False)
                        mm(yb[po, P:T], vtok[:, 1, g * HD:(g + 1) * HD], PT[g % 2][:, T:3 * P], False, True)\
                            .then_inc(S("pv_mm"), 1)
                pe.wait_ge(S("conv_done"), l + 1)
                for c in range(2):
                    m = mm(bank[3][:, 0:T], k("ones"), yconv[:, c, :], c == 0, c == 1)
                m.then_inc(S("ln_sum"), 1)
                pe.wait_ge(S("ln_sq"), l + 1)
                for c in range(2):
                    m = mm(bank[3][:, 0:T], k("ones"), sqc[:, c, :], c == 0, c == 1)
                m.then_inc(S("ln_var"), 1)
                pe.wait_ge(S("y_ev"), 4 * (l + 1))
                pe.wait_ge(S("ln_out"), 2 * (l + 1))
                pe.wait_ge(S("rnn_out"), l + 1)
                for m_ in range(N_OUT):
                    if m_ >= 4:
                        pe.wait_ge(S("op_ev"), N_OUT * l + m_ - 3)
                    feature_tile(t0 + N_IN + m_, bank[m_ % 4][:, 0:T], mixT)
                norm_sums(f"n2.{l}")
                pe.wait_ge(S("norm_out"), NORMS.index(f"n2.{l}") + 1)
                pe.wait_ge(S("keys_in"), 16 * (l + 1))
                for j in range(N_WQ + 1):
                    if j < N_WQ:
                        if j >= 2:
                            pe.wait_ge(S("qs_ev"), N_WQ * l + j - 1)
                        feature_tile(t0 + N_IN + N_OUT + j, bank[j % 2][:, 0:T], Hx)
                    if j >= 1:
                        i = j - 1
                        pe.wait_ge(S("qs_ev"), N_WQ * l + i + 1)
                        if i >= 2:
                            pe.wait_ge(S("top_ev"), N_WQ * l + i - 1)
                        for tt in range(2):
                            m = mm(bank[2 + i % 2][:, tt * P:(tt + 1) * P], qs[i % 2][:, tt * P:(tt + 1) * P],
                                   keysT[:, i, :], True, True)
                        m.then_inc(S("s_mm"), 1)
                p0 = t0 + N_IN + N_OUT + N_WQ
                for i in range(4):
                    mm(bank[4 + i][:, :], zero[:, :], K[:, 0:512], True, False)
                for pi, (kind, q, qb) in enumerate(PHASES):
                    base = p0 + pi * EQ
                    if kind == "v":
                        pe.wait_ge(S("gm_ev"), NKEY * l + (q + 1) * EQ)
                    if pi == 1:
                        for tt in range(2):
                            pe.wait_ge(S("gate_ready"), 2 * l + tt + 1)
                            for i in range(3):
                                m = nc.tensor.transpose(bank[2 + tt][:, i * P:(i + 1) * P], gte[:, tt, i, :], ident)
                            m.then_inc(S("gt_mm"), 1)
                        pe.wait_ge(S("gt_ev"), 2 * (l + 1))

                    def body(it, kind=kind, q=q, qb=qb, base=base):
                        for s in range(R):
                            if kind == "u":
                                pe.wait_ge(S("h_ev"), NKEY * l + q * EQ + s + 1 + R * it)
                                feature_tile(base + s, bank[s % 2][:, 0:T], Hx, it)
                            else:
                                w = tile_ready(base + s, it)
                                g = GH[q % 2][:, bass.ds(it * R + s, 1), :].rearrange("p o t -> p (o t)")
                                for m_ in range(C):
                                    m = mm(bank[4 + m_ // 2][:, (m_ % 2) * T:(m_ % 2 + 1) * T], w[:, m_, :], g, False, False)
                                m.then_inc(S("tile_done"), 1)
                            if qb is not None:
                                n = NKEY * l + qb * EQ + s + R * it
                                pe.wait_ge(S("a_ready"), n + 1)
                                pe.wait_ge(S("b_ready"), n + 1)
                                after(pe, S("gm_ev"), n - 1)
                                for i in range(BT):
                                    m = mm(bank[2 + s % 2][:, i * EQ:(i + 1) * EQ], Aoh[s % 2][:, i, :],
                                           Bg[s % 2][:, i, :], True, True)
                                m.then_inc(S("g_mm"), 1)

                    steps(pe, EQ // R, l == 0 and pi == 1, body)
                for i in range(4):
                    m = mm(bank[4 + i][:, :], zero[:, :], K[:, 0:512], False, True)
                m.then_inc(S("acc_done"), 1)
            norm_sums("fin")

            def group_sum(j, srcs, ones_, width):
                pe.wait_ge(S("gn_sq"), j + 1)
                if j >= 4:
                    pe.wait_ge(S("gn_rt"), j - 3)
                for n in range(srcs):
                    m = mm(bank[4 + j % 4][:, 0:width], ones_, sqg[j % 2][:, n, 0:width], n == 0, n == srcs - 1)
                m.then_inc(S("gn_ss"), 1)

            def transpose_and_apply(n, nk, oslice, vals, width):
                pe.wait_ge(S("u_p"), n + 1)
                if n >= 2:
                    pe.wait_ge(S("u_ptev"), n - 1)
                for i in range(nk):
                    m = nc.tensor.transpose(bank[4 + n % 2][:, i * P:(i + 1) * P], Pb[n % 2][:, 0, i * P:(i + 1) * P], ident)
                m.then_inc(S("u_pt"), 1)
                pe.wait_ge(S("u_ptev"), n + 1)
                for i in range(nk):
                    m = mm(oslice, vals(i), AT[n % 2][:, i, :], i == 0, i == nk - 1)
                m.then_inc(S("u_pv"), 1)

            pe.wait_ge(S("lam_prod"), 1)
            mm(bank[6][:, 0:2], k("ones"), col[:, 60:62], True, True).then_inc(S("lam_mm"), 1)
            for l in range(L):
                b0 = SB[l]
                b1 = b0 + N_MOD
                b2 = b1 + PROJ[l]
                b3 = b2 + N_OUT
                b4 = b3 + N_FIN
                xs = slice(0, T2) if l == 0 else XS
                w_ = T2 if l == 0 else T
                pe.wait_ge(S("csil"), 1)
                if l == 1:
                    pe.wait_ge(S("res_ev"), 2 * C)

                def mod_body(it):
                    for s in range(R):
                        w = tile_ready(b0 + s, it)
                        for c in range(C):
                            m = mm(bank[5][:, bass.ds(it * (2 * R) + 2 * s, 2)], w[:, c, :], csil[:, c, :], c == 0, c == C - 1)
                        m.then_inc(S("tile_done"), 1)

                steps(pe, N_MOD // R, False, mod_body)
                norm_sums(f"a{l}", T2)
                pe.wait_ge(S("norm_add"), (32 if l else 0) + 16)
                if l == 0:
                    for i in range(16):
                        if i >= 4:
                            pe.wait_ge(S("pj_ev"), i - 3)
                        if i < 12:
                            feature_tile(b1 + i, bank[i % 4][:, :], H)
                        else:
                            w = tile_ready(b1 + i)
                            for tt in range(4):
                                for c in range(C):
                                    m = mm(bank[i % 4][:, tt * P:(tt + 1) * P], H[:, c, tt * P:(tt + 1) * P], w[:, c, :],
                                           c == 0, c == C - 1)
                            m.then_inc(S("tile_done"), 1)
                        j = i - 3
                        if 0 <= j < 11:
                            group_sum(j, 2 if j == 8 else 1, k("half") if j < 8 else k("ones"), T2)
                    pe.wait_ge(S("mla_in"), 16)
                    pe.wait_ge(S("gn_out"), 11)
                    for o in range(16):
                        pe.wait_ge(S("pj_ev"), 16 + o - 3)
                        if o < 8:
                            for c in range(2):
                                m = mm(bank[o % 4][:, :], mlaw[:, 2 * o + c, :], raw[:, 8 + c, :], c == 0, c == 1)
                        elif o < 12:
                            m = mm(bank[o % 4][:, :], mlaw[:, 8 + o, :], raw[:, 10, :], True, True)
                        else:
                            for tt in range(4):
                                m = mm(bank[o % 4][:, tt * P:(tt + 1) * P], raw[:, 10, tt * P:(tt + 1) * P],
                                       mlaw[:, 8 + o, :], True, True)
                        m.then_inc(S("p2_mm"), 1)
                    for j in range(8):
                        group_sum(G_MLA + j, 2 if j < 4 else 1, k("ones"), T2)
                    pe.wait_ge(S("pj_ev"), 32)
                    pe.wait_ge(S("gn_out"), G_DA)
                    for r_, t_ in enumerate(rope_tiles):
                        if r_ >= 4:
                            pe.wait_ge(S("rope_ev"), r_ - 3)
                        mm(bank[r_ % 4][:, 0:T], k("rot"), t_[:, XS], True, True).then_inc(S("rope_mm"), 1)
                    pe.wait_ge(S("rope_out"), len(rope_tiles))
                    for n in range(33):
                        if n < 32:
                            hh, qt = n // 4, n % 4
                            nk = 2 * P if qt < 2 else T2
                            qsl = slice(qt * P, (qt + 1) * P)
                            if n >= 2:
                                pe.wait_ge(S("u_exp"), n - 1)
                            sb_ = 2 * (n % 2)
                            if hh < 4:
                                for i in range(2):
                                    po = slice(64 * i, 64 * i + 64)
                                    m = mm(bank[sb_ + i][:, 0:nk], raw[po, hh, qsl], raw[po, 4 + hh, 0:nk], True, True)
                            else:
                                h = hh - 4
                                mm(bank[sb_][:, 0:nk], raw2[:, 2 * h, qsl], raw2[:, 8 + h, 0:nk], True, False)
                                m = mm(bank[sb_][:, 0:nk], raw2[:, 2 * h + 1, qsl], raw[:, 11, 0:nk], False, True)
                            m.then_inc(S("u_mm"), 1)
                        if n >= 1:
                            g = n - 1
                            hh, qt = g // 4, g % 4
                            if hh >= 2 and qt == 0:
                                pe.wait_ge(S("o_ev"), hh - 1)
                            vals = vda if hh < 4 else vml
                            transpose_and_apply(g, 2 if qt < 2 else 4, bank[6 + hh % 2][:, qt * P:(qt + 1) * P],
                                                lambda i, vals=vals, h=hh % 4: vals[:, i, h * P:(h + 1) * P], T2)
                    pe.wait_ge(S("o_ev"), 8)
                    for h in range(4):
                        group_sum(G_DA + h, 1, k("ones"), T2)
                    pe.wait_ge(S("gn_out"), G_NA)
                    mixer_out = mix2
                else:
                    for i in range(24):
                        if i >= 4:
                            pe.wait_ge(S("pj_ev"), 32 + i - 3)
                        if i < 8:
                            feature_tile(b1 + i, bank[i % 4][:, 0:T], Hx)
                        elif i < 16:
                            feature_tile(b1 + i, bank[i % 4][:, :], H)
                        else:
                            w = tile_ready(b1 + i)
                            for tt in range(4):
                                for c in range(C):
                                    m = mm(bank[i % 4][:, tt * P:(tt + 1) * P], H[:, c, tt * P:(tt + 1) * P], w[:, c, :],
                                           c == 0, c == C - 1)
                            m.then_inc(S("tile_done"), 1)
                        j = i - 3
                        if 0 <= j < 16:
                            group_sum(G_NA + j, 1, k("half"), T if j < 8 else T2)
                    pe.wait_ge(S("gn_out"), G_NA + 16)
                    pe.wait_ge(S("pj_ev"), 32 + 24)
                    for n in range(32, 65):
                        if n < 64:
                            h, qt = (n - 32) // 2, n % 2
                            po = slice(64 * (h % 2), 64 * (h % 2) + 64)
                            if n >= 34:
                                pe.wait_ge(S("u_sc"), n - 32 - 1)
                            mm(bank[2 * (n % 2)][:, :], qN[po, h // 2, qt * P:(qt + 1) * P], kN[po, h // 2, :], True, True)\
                                .then_inc(S("u_mm"), 1)
                        if n >= 33:
                            g = n - 1
                            h, qt = (g - 32) // 2, g % 2
                            hc = h // 2
                            po = slice(64 * (h % 2), 64 * (h % 2) + 64)
                            if hc >= 2 and h % 2 == 0 and qt == 0:
                                pe.wait_ge(S("o_ev"), 8 + hc - 1)
                            transpose_and_apply(g, 4, bank[6 + hc % 2][po, qt * P:(qt + 1) * P],
                                                lambda i, h=h: vN[:, i, h * HD:(h + 1) * HD], T)
                    pe.wait_ge(S("o_ev"), 16)
                    mixer_out = mix2[:, :, XS]
                for m_ in range(C):
                    if m_ >= 4:
                        pe.wait_ge(S("res_ev"), 2 * C * l + m_ - 3)
                    feature_tile(b2 + m_, bank[m_ % 4][:, 0:w_], mixer_out)
                norm_sums(f"f{l}", w_)
                pe.wait_ge(S("norm_add"), (48 if l else 16) + (8 if l else 16))
                Hf = H[:, :, xs]
                for m_ in range(KF):
                    if m_ >= 2:
                        pe.wait_ge(S("hid"), KF * l + m_ - 1)
                    for g in range(2):
                        feature_tile(b3 + 2 * m_ + g, bank[2 * (m_ % 2) + g][:, 0:w_], Hf)
                pe.wait_ge(S("hid"), KF * (l + 1))
                for half in range(2):
                    for j in range(KF // 2):
                        w = tile_ready(b4 + half * (KF // 2) + j)
                        for kk in range(2):
                            for m_ in range(4):
                                m = mm(bank[4 * (1 - half) + m_][:, 0:w_], w[:, 4 * kk + m_, :], hid[:, 2 * j + kk, 0:w_],
                                       j == 0 and kk == 0, j == KF // 2 - 1 and kk == 1)
                        m.then_inc(S("tile_done"), 1)

        @block.scalar
        def _(act):
            def norm_act(name, x, width, sems_):
                j = NORMS.index(name)
                for s_, v_ in sems_:
                    act.wait_ge(s_, v_)
                nc.scalar.activation(sq[:, :, 0:width], x, ACT.Square).then_inc(S("norm_sq"), 1)
                act.wait_ge(S("norm_ss"), j + 1)
                nc.scalar.activation(rt[:, 0:width], bank[7][:, 0:width], ACT.Sqrt, bias=eps[:, :],
                                     scale=1.0 / D).then_inc(S("norm_rt"), 1)

            act.wait_ge(S("setup"), 1)
            for _i in range(2):
                nc.scalar.copy(col[:, 90 + _i:91 + _i], eps[:, :]).then_inc(S("h_ev"), 1)
            for l in range(L):
                norm_act(f"n1.{l}", X[:, :, XS], T,
                         [(S("x_in"), 16)] if l == 0 else [(S("peer_out"), l)])
                act.wait_ge(S("fz_ready"), l + 1)
                nc.scalar.activation(fz[1][0:HEADS, :], fz[2][0:HEADS, :], ACT.Exp, scale=-1.0).then_inc(S("fexp"), 1)
                act.wait_ge(S("lam_abs"), l + 1)
                nc.scalar.activation(col[:, 2:4], col[:, 0:2], ACT.Exp, scale=-1.0).then_inc(S("lamexp"), 1)

                def evac(i, out, src, func=ACT.Copy, scale=1.0):
                    act.wait_ge(S("tile_done"), l * N1 + i + 1)
                    nc.scalar.activation(out, src, func, scale=scale).then_inc(S("proj_ev"), 1)

                for i in range(16):
                    b = bank[i % 4][:, 0:T]
                    if i < 2:
                        evac(i, cvA[:, i, :], b)
                    elif i < 4:
                        evac(i, cvG[:, i - 2, :], b, ACT.Sigmoid)
                    elif i < 6:
                        if i == 4:
                            act.wait_ge(S("pads"), l + 1)
                        evac(i, rpad[:, i - 4, RTAPS - 1:], b)
                    elif i < 8:
                        evac(i, gateG[:, i - 6, :], b, ACT.Gelu_apprx_tanh)
                    elif i < 12:
                        evac(i, qT[:, i - 8, :], b, scale=0.125)
                    else:
                        evac(i, kT[:, i - 12, :], b)
                    if i == 11:
                        act.wait_ge(S("rg_mm"), l + 1)
                        for c in range(2):
                            nc.scalar.activation(rg[:, c, :], bank[5][:, c * T:(c + 1) * T], ACT.Sigmoid,
                                                 bias=k(f"br{l}", c, c + 1))
                            m = nc.scalar.activation(ig[:, c, :], bank[6][:, c * T:(c + 1) * T], ACT.Sigmoid,
                                                     bias=k(f"bi{l}", c, c + 1))
                            m.then_inc(S("rg_ev"), 1)
                for n in range(4):
                    evac(16 + n, vtok[:, :, n * P:(n + 1) * P],
                         bank[n][:, 0:T].rearrange("p (a b) -> p a b", a=2))
                act.wait_ge(S("loga"), l + 1)
                nc.scalar.activation(aa[:, :, :], la[:, :, :], ACT.Exp).then_inc(S("rnn_exp"), 1)
                nc.scalar.activation(th[:, :, :], la[:, :, :], ACT.Tanh, scale=-1.0).then_inc(S("rnn_exp"), 1)
                act.wait_ge(S("m2_ready"), l + 1)
                nc.scalar.activation(m2[:, :, :], m2[:, :, :], ACT.Sqrt).then_inc(S("rnn_root"), 1)
                for h in range(HEADS + 1):
                    if h < HEADS:
                        act.wait_ge(S("att_mx"), HEADS * l + h + 1)
                        if h >= 2:
                            act.wait_ge(S("pt_mm"), HEADS * l + h - 1)
                        nm = col[:, 8 + 2 * (h % 2):10 + 2 * (h % 2)]
                        sm = col[:, 12 + 2 * (h % 2):14 + 2 * (h % 2)]
                        nc.scalar.activation(Pm[h % 2][:, 0:P], sc[h % 2][:, 0:P], ACT.Exp, bias=nm[:, 0:1],
                                             accum_out=sm[:, 0:1])
                        nc.scalar.activation(Pm[h % 2][:, P:], sc[h % 2][:, P:], ACT.Exp, bias=nm[:, 1:2],
                                             accum_out=sm[:, 1:2]).then_inc(S("att_exp"), 1)
                    if h >= 1:
                        g = h - 1
                        act.wait_ge(S("pt_mm"), HEADS * l + g + 1)
                        if g >= 2:
                            act.wait_ge(S("pv_mm"), HEADS * l + g - 1)
                        nc.scalar.copy(PT[g % 2][:, :], bank[6 + g % 2][:, 0:3 * P]).then_inc(S("pt_ev"), 1)
                        if g % 2:
                            act.wait_ge(S("pv_mm"), HEADS * l + g + 1)
                            nc.scalar.copy(mixT[:, g // 2, :], bank[(g // 2) % 2][:, 0:T]).then_inc(S("y_ev"), 1)
                act.wait_ge(S("ln_cen"), l + 1)
                nc.scalar.activation(sqc[:, :, :], cen[:, :, :], ACT.Square).then_inc(S("ln_sq"), 1)
                act.wait_ge(S("ln_var"), l + 1)
                nc.scalar.activation(rt[:, 0:T], bank[3][:, 0:T], ACT.Sqrt, bias=eps[:, :], scale=1.0 / 256)\
                    .then_inc(S("ln_root"), 1)
                act.wait_ge(S("ln_z"), l + 1)
                for c in range(2):
                    nc.scalar.activation(mixT[:, 4 + c, :], cen[:, c, :], ACT.Silu, bias=k(f"lb{l}", c, c + 1))\
                        .then_inc(S("ln_out"), 1)
                norm_act(f"n2.{l}", X[:, :, XS], T, [(S("op_ev"), N_OUT * (l + 1))])
                for j in range(N_WQ):
                    act.wait_ge(S("tile_done"), l * N1 + N_IN + N_OUT + j + 1)
                    if j >= 2:
                        act.wait_ge(S("s_mm"), N_WQ * l + j - 1)
                    nc.scalar.copy(qs[j % 2][:, :], bank[j % 2][:, 0:T]).then_inc(S("qs_ev"), 1)
                p0 = l * N1 + N_IN + N_OUT + N_WQ
                for pi, (kind, q, qb) in enumerate(PHASES):
                    if pi == 1:
                        for tt in range(2):
                            act.wait_ge(S("sv_sub"), 2 * l + tt + 1)
                            nc.scalar.activation(gte[:, tt, 0, :], sv[:, tt, :, :].rearrange("p a b -> p (a b)"), ACT.Exp)\
                                .then_inc(S("sv_exp"), 1)
                    if kind == "v":
                        continue
                    base = p0 + pi * EQ
                    if q >= 2:
                        act.wait_ge(S("tile_done"), p0 + (PHASES.index(("v", q - 2, None)) + 1) * EQ)

                    def body(it, q=q, base=base):
                        for s in range(R):
                            act.wait_ge(S("tile_done"), base + s + 1 + R * it)
                            act.wait_ge(S("const_in"), 16)
                            o = GH[q % 2][:, bass.ds(it * R + s, 1), :].rearrange("p o t -> p (o t)")
                            nc.scalar.activation(o, bank[s % 2][:, 0:T], ACT.Gelu_apprx_tanh).then_inc(S("h_ev"), 1)

                    steps(act, EQ // R, False, body)
            norm_act("fin", X[:, :, XS], T, [(S("peer_out"), L)])

            nc.scalar.activation(csil, k("cc").rearrange("p (a b) -> p a b", a=C), ACT.Silu).then_inc(S("csil"), 1)
            act.wait_ge(S("lam_mm"), 1)
            nc.scalar.activation(col[:, 62:64], bank[6][:, 0:2], ACT.Exp).then_inc(S("lam_exp"), 1)

            def squares(j, srcs, width, bufs=2):
                if j >= 2:
                    act.wait_ge(S("gn_ss"), j - 1)
                for n, s_ in enumerate(srcs):
                    m = nc.scalar.activation(sqg[j % 2][:, n, 0:width], s_, ACT.Square)
                m.then_inc(S("gn_sq"), 1)

            def group_root(j, count, width):
                act.wait_ge(S("gn_ss"), j + 1)
                if j >= 4:
                    act.wait_ge(S("gn_out"), j - 3)
                nc.scalar.activation(grt[j % 4][:, 0:width], bank[4 + j % 4][:, 0:width], ACT.Sqrt, bias=eps[:, :],
                                     scale=1.0 / count).then_inc(S("gn_rt"), 1)

            def unit_out(n, nk):
                act.wait_ge(S("u_pt"), n + 1)
                if n >= 2:
                    act.wait_ge(S("u_pv"), n - 1)
                nc.scalar.copy(AT[n % 2][:, 0:nk, :], bank[4 + n % 2][:, 0:nk * P].rearrange("p (a b) -> p a b", b=P))\
                    .then_inc(S("u_ptev"), 1)

            def norm_shift(l, base, halves, sh):
                n = base
                for c in range(C):
                    for s_ in halves:
                        n += 1
                        act.wait_ge(S("norm_mul"), n)
                        xs = slice(s_ * T, (s_ + 1) * T)
                        nc.scalar.activation(H[:, c, xs], H[:, c, xs], ACT.Identity, bias=modv[l][:, sh * C + c, s_:s_ + 1])\
                            .then_inc(S("norm_add"), 1)

            for l in range(L):
                b0 = SB[l]
                b1 = b0 + N_MOD
                b2 = b1 + PROJ[l]
                b3 = b2 + N_OUT
                w_ = T2 if l == 0 else T
                xs = slice(0, T2) if l == 0 else XS
                norm_act(f"a{l}", X[:, :, :], T2, [(S("ctx_in"), 16), (S("norm_out"), 5)] if l == 0 else [(S("res_ev"), 2 * C)])
                norm_shift(l, 32 * l, (0, 1), 0)
                if l == 0:
                    srcs = [[raw[:, i, :]] for i in range(8)] + [[raw[:, 8, :], raw[:, 9, :]], [raw[:, 10, :]], [raw[:, 11, :]]]
                    counts = [64] * 8 + [256, 128, 64]
                    for i in range(16):
                        act.wait_ge(S("tile_done"), b1 + i + 1)
                        if i < 12:
                            nc.scalar.copy(raw[:, i, :], bank[i % 4][:, :]).then_inc(S("pj_ev"), 1)
                        else:
                            nc.scalar.copy(vda[:, :, (i - 12) * P:(i - 11) * P],
                                           bank[i % 4][:, :].rearrange("p (a b) -> p a b", a=4)).then_inc(S("pj_ev"), 1)
                        if 1 <= i < 12:
                            act.wait_ge(S("pj_ev"), i + 1)
                            squares(i - 1, srcs[i - 1], T2)
                        if 0 <= i - 3 < 11:
                            group_root(i - 3, counts[i - 3], T2)
                    for o in range(16):
                        act.wait_ge(S("p2_mm"), o + 1)
                        if o < 12:
                            nc.scalar.copy(raw2[:, o, :], bank[o % 4][:, :]).then_inc(S("pj_ev"), 1)
                        else:
                            nc.scalar.copy(vml[:, :, (o - 12) * P:(o - 11) * P],
                                           bank[o % 4][:, :].rearrange("p (a b) -> p a b", a=4)).then_inc(S("pj_ev"), 1)
                    act.wait_ge(S("pj_ev"), 32)
                    for j in range(9):
                        if j < 8:
                            squares(G_MLA + j, [raw2[:, 2 * j, :], raw2[:, 2 * j + 1, :]] if j < 4 else [raw2[:, 4 + j, :]], T2)
                        if j >= 1:
                            group_root(G_MLA + j - 1, 192 if j - 1 < 4 else 128, T2)
                    for n in range(33):
                        if n < 32:
                            hh, qt = n // 4, n % 4
                            nk = 2 * P if qt < 2 else T2
                            act.wait_ge(S("u_mx"), n + 1)
                            if n >= 2:
                                act.wait_ge(S("u_pt"), n - 1)
                            a0 = 24 + 4 * (n % 2)
                            for i in range(2 if hh < 4 else 1):
                                m = nc.scalar.activation(Pb[n % 2][:, i, 0:nk], bank[2 * (n % 2) + i][:, 0:nk], ACT.Exp,
                                                         bias=col[:, a0 + i:a0 + i + 1],
                                                         accum_out=col[:, a0 + 2 + i:a0 + 3 + i])
                            m.then_inc(S("u_exp"), 1)
                        if n >= 1:
                            g = n - 1
                            unit_out(g, 2 if g % 4 < 2 else 4)
                            if g % 4 == 3:
                                act.wait_ge(S("u_pv"), g + 1)
                                nc.scalar.copy(mix2[:, g // 4, :], bank[6 + (g // 4) % 2][:, :]).then_inc(S("o_ev"), 1)
                    act.wait_ge(S("o_ev"), 8)
                    for j in range(5):
                        if j < 4:
                            squares(G_DA + j, [mix2[:, j, :]], T2)
                        if j >= 1:
                            group_root(G_DA + j - 1, 128, T2)
                else:
                    for i in range(24):
                        act.wait_ge(S("tile_done"), b1 + i + 1)
                        if i < 8:
                            nc.scalar.copy(qN[:, i, :], bank[i % 4][:, 0:T]).then_inc(S("pj_ev"), 1)
                        elif i < 16:
                            nc.scalar.copy(kN[:, i - 8, :], bank[i % 4][:, :]).then_inc(S("pj_ev"), 1)
                        else:
                            nc.scalar.copy(vN[:, :, (i - 16) * P:(i - 15) * P],
                                           bank[i % 4][:, :].rearrange("p (a b) -> p a b", a=4)).then_inc(S("pj_ev"), 1)
                        if 1 <= i < 17:
                            j = i - 1
                            act.wait_ge(S("pj_ev"), 32 + i)
                            squares(G_NA + j, [qN[:, j, :] if j < 8 else kN[:, j - 8, :]], T if j < 8 else T2)
                        if 0 <= i - 3 < 16:
                            group_root(G_NA + i - 3, 64, T if i - 3 < 8 else T2)
                    for n in range(32, 65):
                        if n < 64:
                            act.wait_ge(S("u_mx"), n + 1)
                            act.wait_ge(S("u_pt"), n - 1)
                            a0 = 24 + 4 * (n % 2)
                            nc.scalar.activation(Pb[n % 2][:, 0, :], Pb[n % 2][:, 1, :], ACT.Exp, bias=col[:, a0:a0 + 1],
                                                 accum_out=col[:, a0 + 2:a0 + 3]).then_inc(S("u_exp"), 1)
                        if n >= 33:
                            g = n - 1
                            unit_out(g, 4)
                            if g % 4 == 3:
                                hc = (g - 32) // 4
                                act.wait_ge(S("u_pv"), g + 1)
                                nc.scalar.copy(mix2[:, hc, XS], bank[6 + hc % 2][:, 0:T]).then_inc(S("o_ev"), 1)
                norm_act(f"f{l}", X[:, :, xs], w_, [(S("res_ev"), 2 * C * l + C)])
                norm_shift(l, 48 if l else 16, (0, 1) if l == 0 else (1,), 3)
                for m_ in range(KF):
                    act.wait_ge(S("tile_done"), b3 + 2 * m_ + 1)
                    if m_ >= 2:
                        act.wait_ge(S("hid"), KF * l + m_ - 1)
                    nc.scalar.activation(sg[m_ % 2][:, 0:w_], bank[2 * (m_ % 2)][:, 0:w_], ACT.Silu).then_inc(S("silu"), 1)

        @block.vector
        def _(dve):
            v = nc.vector
            order = [0]

            def link(ins):
                order[0] += 1
                ins.then_inc(S("dve_order"), 1)
                return order[0]

            def seq(ins):
                dve.wait_ge(S("dve_order"), link(ins))

            def norm_out(name, x, width, gains, out, shifts=None):
                j = NORMS.index(name)
                dve.wait_ge(S("norm_rt"), j + 1)
                seq(v.reciprocal(rs[:, 0:width], rt[:, 0:width]))
                for c in range(C):
                    m = v.scalar_tensor_tensor(out=out[:, c, :], in0=x[:, c, :], scalar=gains[:, c:c + 1],
                                               in1=rs[:, 0:width], op0=ALU.mult, op1=ALU.mult)
                m.then_inc(S("norm_out"), 1)

            def log1p(u, s1, s2, acc):
                seq(v.tensor_scalar(s1, u, 2.0, None, ALU.add))
                seq(v.reciprocal(s1, s1))
                seq(v.tensor_tensor(s1, u, s1, ALU.mult))
                seq(v.tensor_tensor(s2, s1, s1, ALU.mult))
                seq(v.tensor_scalar(acc, s2, 1.0 / 15, None, ALU.mult))
                for n in (13, 11, 9, 7, 5, 3):
                    seq(v.scalar_tensor_tensor(out=acc, in0=acc, scalar=1.0 / n, in1=s2, op0=ALU.add, op1=ALU.mult))
                seq(v.scalar_tensor_tensor(out=acc, in0=acc, scalar=1.0, in1=s1, op0=ALU.add, op1=ALU.mult))

            v.memset(zero[:, :], 0.0).then_inc(S("setup0"), 1)
            dve.wait_ge(S("setup0"), 1)
            v.memset(eps[:, :], EPS).then_inc(S("setup"), 1)
            dve.wait_ge(S("const_in"), 16)
            for l in range(L):
                norm_out(f"n1.{l}", X[:, :, XS], T, k(f"g1_{l}"), H[:, :, XS])
                z, u, za = fz[0][0:HEADS, :], fz[1][0:HEADS, :], fz[2][0:HEADS, :]
                dve.wait_ge(S("f_mm"), l + 1)
                seq(v.tensor_scalar(z, bank[4][0:HEADS, 0:T], k(f"bf{l}")[0:HEADS, :], None, ALU.add))
                v.scalar_tensor_tensor(out=za, in0=z, scalar=-1.0, in1=z, op0=ALU.mult, op1=ALU.max).then_inc(S("fz_ready"), 1)
                lam = k(f"lam{l}")
                v.scalar_tensor_tensor(out=col[:, 0:2], in0=lam, scalar=-1.0, in1=lam, op0=ALU.mult, op1=ALU.max).then_inc(S("lam_abs"), 1)
                v.memset(ypad[:, :, 0:TAPS - 1], 0.0)
                m = v.memset(rpad[:, :, 0:RTAPS - 1], 0.0)
                m.then_inc(S("pads"), 1)
                seq(v.tensor_copy(sel[0:HEADS, :, :], ident[0:HEADS, 0:HEADS].unsqueeze(2).broadcast_to([HEADS, HEADS, P])))
                dve.wait_ge(S("fexp"), l + 1)
                log1p(u, fz[3][0:HEADS, :], fz[4][0:HEADS, :], fz[5][0:HEADS, :])
                seq(v.tensor_scalar(z, z, 0.0, None, ALU.min))
                seq(v.scalar_tensor_tensor(out=z, in0=fz[5][0:HEADS, :], scalar=-2.0, in1=z, op0=ALU.mult, op1=ALU.add))
                seq(v.memset(fz[3][0:HEADS, :], 1.0))
                seq(v.tensor_tensor_scan(cum[0:HEADS, :], fz[3][0:HEADS, :], z, 0.0, ALU.mult, ALU.add))
                v.tensor_scalar(ncum[0:HEADS, :], cum[0:HEADS, :], -1.0, None, ALU.mult).then_inc(S("cum_ready"), 1)
                dve.wait_ge(S("lamexp"), l + 1)
                log1p(col[:, 2:4], col[:, 4:6], col[:, 6:8], col[:, 16:18])
                seq(v.tensor_scalar(col[:, 18:20], lam, -1.0, 0.0, ALU.mult, ALU.max))
                seq(v.scalar_tensor_tensor(out=col[:, 18:20], in0=col[:, 16:18], scalar=2.0, in1=col[:, 18:20],
                                           op0=ALU.mult, op1=ALU.add))
                seq(v.tensor_scalar(col[:, 20:22], col[:, 18:20], -8.0, None, ALU.mult))
                dve.wait_ge(S("proj_ev"), N_IN * l + 4)
                seq(v.tensor_tensor(ypad[:, :, TAPS - 1:], cvA[:, :, :], cvG[:, :, :], ALU.mult))
                dve.wait_ge(S("proj_ev"), N_IN * l + 6)

                def conv(out, src, taps, w, b):
                    last = [0, 0]
                    for j in range(taps):
                        for c in range(2):
                            if j == 0:
                                last[c] = link(v.tensor_scalar(out[:, c, :], src[:, c, 0:T], w[:, c * taps:c * taps + 1],
                                                               b[:, c:c + 1], ALU.mult, ALU.add))
                            else:
                                dve.wait_ge(S("dve_order"), last[c])
                                last[c] = link(v.scalar_tensor_tensor(
                                    out=out[:, c, :], in0=src[:, c, j:j + T], scalar=w[:, c * taps + j:c * taps + j + 1],
                                    in1=out[:, c, :], op0=ALU.mult, op1=ALU.add))
                    dve.wait_ge(S("dve_order"), last[1])

                conv(xr, rpad, RTAPS, k(f"rw{l}"), k(f"rb{l}"))
                dve.nop().then_inc(S("xr_ready"), 1)
                conv(yconv, ypad, TAPS, k(f"cw{l}"), k(f"cb{l}"))
                dve.nop().then_inc(S("conv_done"), 1)
                dve.wait_ge(S("rg_ev"), 2 * l + 2)
                for c in range(2):
                    m = v.tensor_scalar(la[:, c, :], rg[:, c, :], col[:, 20 + c:21 + c], None, ALU.mult)
                m.then_inc(S("loga"), 1)
                seq(v.tensor_tensor(bx[:, :, :], ig[:, :, :], xr[:, :, :], ALU.mult))
                dve.wait_ge(S("rnn_exp"), 2 * l + 2)
                seq(v.tensor_tensor(m2[:, :, :], aa[:, :, :], aa[:, :, :], ALU.mult))
                v.scalar_tensor_tensor(out=m2[:, :, :], in0=m2[:, :, :], scalar=1.0, in1=th[:, :, :],
                                       op0=ALU.add, op1=ALU.mult).then_inc(S("m2_ready"), 1)
                dve.wait_ge(S("rnn_root"), l + 1)
                seq(v.tensor_tensor(bx[:, :, :], bx[:, :, :], m2[:, :, :], ALU.mult))
                for c in range(2):
                    n = link(v.tensor_tensor_scan(hs[:, c, :], aa[:, c, :], bx[:, c, :], 0.0, ALU.mult, ALU.add))
                dve.wait_ge(S("dve_order"), n)
                v.tensor_tensor(mixT[:, 6:8, :], hs[:, :, :], gateG[:, :, :], ALU.mult).then_inc(S("rnn_out"), 1)
                dve.wait_ge(S("bc_mm"), l + 1)
                v.tensor_copy(cT[:, :, :], bank[5][:, 0:2 * HEADS].rearrange("p (a b) -> p a b", a=2))
                for i in range(4):
                    src = bank[(0, 1, 2, 4)[i]][:, :].rearrange("p (a b) -> p a b", a=2)
                    mk = k("mask").unsqueeze(1).broadcast_to([P, 2, P])
                    dst = biasT[:, 2 * i:2 * i + 2, :]
                    v.tensor_tensor(dst[:, :, 0:P], src[:, :, 0:P], mk, ALU.add)
                    v.tensor_copy(dst[:, :, P:2 * P], src[:, :, 0:P])
                    m = v.tensor_tensor(dst[:, :, 2 * P:], src[:, :, P:], mk, ALU.add)
                m.then_inc(S("bc_ev"), 1)
                dve.wait_ge(S("bc_ev"), l + 1)
                for h in range(HEADS + 1):
                    if h < HEADS:
                        dve.wait_ge(S("att_mm"), HEADS * l + h + 1)
                        if h >= 2:
                            dve.wait_ge(S("att_exp"), HEADS * l + h - 1)
                        s_, b = sc[h % 2], bank[4 + h % 2]
                        v.scalar_tensor_tensor(out=s_[:, 0:P], in0=b[:, 0:P], scalar=cT[:, 0, h:h + 1],
                                               in1=biasT[:, h, 0:P], op0=ALU.add, op1=ALU.add)
                        v.scalar_tensor_tensor(out=s_[:, P:], in0=b[:, P:3 * P], scalar=cT[:, 1, h:h + 1],
                                               in1=biasT[:, h, P:], op0=ALU.add, op1=ALU.add).then_inc(S("att_sc"), 1)
                        dve.wait_ge(S("att_sc"), HEADS * l + h + 1)
                        nm = col[:, 8 + 2 * (h % 2):10 + 2 * (h % 2)]
                        v.tensor_reduce(nm[:, 0:1], s_[:, 0:P], AXX, ALU.max, negate=True)
                        v.tensor_reduce(nm[:, 1:2], s_[:, P:], AXX, ALU.max, negate=True).then_inc(S("att_mx"), 1)
                    if h >= 1:
                        g = h - 1
                        dve.wait_ge(S("att_exp"), HEADS * l + g + 1)
                        sm = col[:, 12 + 2 * (g % 2):14 + 2 * (g % 2)]
                        seq(v.reciprocal(sm, sm))
                        v.tensor_scalar(Pm[g % 2][:, 0:P], Pm[g % 2][:, 0:P], sm[:, 0:1], None, ALU.mult)
                        v.tensor_scalar(Pm[g % 2][:, P:], Pm[g % 2][:, P:], sm[:, 1:2], None, ALU.mult)\
                            .then_inc(S("p_ready"), 1)
                dve.wait_ge(S("ln_sum"), l + 1)
                for c in range(2):
                    m = v.scalar_tensor_tensor(out=cen[:, c, :], in0=bank[3][:, 0:T], scalar=-1.0 / 256,
                                               in1=yconv[:, c, :], op0=ALU.mult, op1=ALU.add)
                m.then_inc(S("ln_cen"), 1)
                dve.wait_ge(S("ln_root"), l + 1)
                seq(v.reciprocal(rs[:, 0:T], rt[:, 0:T]))
                for c in range(2):
                    m = v.scalar_tensor_tensor(out=cen[:, c, :], in0=cen[:, c, :], scalar=k(f"lg{l}", c, c + 1),
                                               in1=rs[:, 0:T], op0=ALU.mult, op1=ALU.mult)
                m.then_inc(S("ln_z"), 1)
                for m_ in range(N_OUT):
                    dve.wait_ge(S("tile_done"), l * N1 + N_IN + m_ + 1)
                    v.tensor_tensor(X[:, m_, XS], X[:, m_, XS], bank[m_ % 4][:, 0:T], ALU.add).then_inc(S("op_ev"), 1)
                norm_out(f"n2.{l}", X[:, :, XS], T, k(f"g2_{l}"), H[:, :, XS])

                def top16(vals, idx, src, scratch):
                    seq(v.max(vals[:, 0:8], src))
                    v.max_index(idx[:, 0:8], vals[:, 0:8], src)
                    seq(v.match_replace(scratch, vals[:, 0:8], src, -3.0e38))
                    seq(v.max(vals[:, 8:16], scratch))
                    return v.max_index(idx[:, 8:16], vals[:, 8:16], scratch)

                for j in range(N_WQ):
                    dve.wait_ge(S("s_mm"), N_WQ * l + j + 1)
                    for tt in range(2):
                        n = link(top16(v12[:, tt, j, :], i12u[:, tt, j, :], bank[2 + j % 2][:, tt * P:(tt + 1) * P], w1[:, :]))
                        dve.wait_ge(S("dve_order"), n)
                    dve.nop().then_inc(S("top_ev"), 1)
                seq(v.tensor_copy(if12[:, :, :, :].rearrange("p a b c -> p (a b c)"),
                                  i12u[:, :, :, :].rearrange("p a b c -> p (a b c)")))
                for tt in range(2):
                    for h in range(PH):
                        seq(v.tensor_tensor(cand[:, :].rearrange("p (a b) -> p a b", a=16),
                                            v12[:, tt, 2 * h, :].unsqueeze(2).broadcast_to([P, 16, 16]),
                                            v12[:, tt, 2 * h + 1, :].unsqueeze(1).broadcast_to([P, 16, 16]), ALU.add))
                        seq(top16(sv[:, tt, h, :], ciu[:, tt, h, :], cand[:, :], cand2[:, :]))
                    cf = ciu[:, tt, :, :].rearrange("p a b -> p (a b)")
                    au = cau[:, tt, :, :].rearrange("p a b -> p (a b)")
                    bu = cbu[:, tt, :, :].rearrange("p a b -> p (a b)")
                    seq(v.tensor_scalar(au, cf, 4, None, ALU.logical_shift_right))
                    seq(v.tensor_scalar(bu, cf, 15, None, ALU.bitwise_and))
                    af = oneh[:, 0, :, :].rearrange("p a b -> p (a b)")
                    seq(v.tensor_copy(af[:, 0:P], au))
                    seq(v.tensor_copy(af[:, P:2 * P], bu))
                    seq(v.tensor_copy(ca[:, tt, :, :].rearrange("p a b -> p (a b)"), af[:, 0:P]))
                    seq(v.tensor_copy(cb[:, tt, :, :].rearrange("p a b -> p (a b)"), af[:, P:2 * P]))
                    for half, rank in ((0, ca), (1, cb)):
                        io = k("iota", 0, 16).unsqueeze(1).unsqueeze(1).broadcast_to([P, 8, 16, 16])
                        seq(v.tensor_tensor(oneh, rank[:, tt, :, :].unsqueeze(3).broadcast_to([P, 8, 16, 16]), io, ALU.is_equal))
                        keys = if12[:, tt, :, :].rearrange("p (h two) s -> p h two s", two=2)[:, :, half, :]
                        seq(v.tensor_tensor(oneh, oneh, keys.unsqueeze(2).broadcast_to([P, 8, 16, 16]), ALU.mult))
                        seq(v.tensor_reduce(gte[:, tt, 1 + half, :].rearrange("p (a b) -> p a b", a=8), oneh, AXX, ALU.add))
                    mx = sv[:, tt, :, 0:1]
                    seq(v.tensor_copy(ssum[:, tt, :].unsqueeze(2), mx))
                    v.tensor_tensor(sv[:, tt, :, :], sv[:, tt, :, :], ssum[:, tt, :].unsqueeze(2).broadcast_to([P, 8, 16]),
                                    ALU.subtract).then_inc(S("sv_sub"), 1)
                for tt in range(2):
                    dve.wait_ge(S("sv_exp"), 2 * l + tt + 1)
                    g3 = gte[:, tt, 0, :].rearrange("p (a b) -> p a b", a=8)
                    seq(v.tensor_reduce(ssum[:, tt, :], g3, AXX, ALU.add))
                    seq(v.reciprocal(ssum[:, tt, :], ssum[:, tt, :]))
                    v.tensor_tensor(g3, g3, ssum[:, tt, :].unsqueeze(2).broadcast_to([P, 8, 16]), ALU.mult)\
                        .then_inc(S("gate_ready"), 1)
                for tt in range(2):
                    dve.wait_ge(S("gt_mm"), 2 * l + tt + 1)
                    v.tensor_copy(gT[:, :, tt * P:(tt + 1) * P], bank[2 + tt][:, 0:3 * P].rearrange("p (a b) -> p a b", a=3))\
                        .then_inc(S("gt_ev"), 1)
                dve.wait_ge(S("gt_ev"), 2 * (l + 1))
                for qb in range(NQ):
                    dve.wait_ge(S("h_ev"), 2 + NKEY * l + (qb + 1) * EQ)

                    def spread(it, s, qb=qb):
                        n = NKEY * l + qb * EQ + s + R * it
                        after(dve, S("g_mm"), n - 1)
                        io = k("iota", qb * EQ, (qb + 1) * EQ).unsqueeze(1).broadcast_to([P, BT, EQ])
                        at = bass.ds(it * (R * BT) + s * BT, BT)
                        v.tensor_tensor(Aoh[s % 2], gT[:, 1, at].unsqueeze(2).broadcast_to([P, BT, P]),
                                        k("iota").unsqueeze(1).broadcast_to([P, BT, P]), ALU.is_equal)\
                            .then_inc(S("a_ready"), 1)
                        v.tensor_tensor(Boh[s % 2], gT[:, 2, at].unsqueeze(2).broadcast_to([P, BT, EQ]), io,
                                        ALU.is_equal).then_inc(S("b_hot"), 1)
                        dve.wait_ge(S("b_hot"), n + 1)
                        v.tensor_tensor(Bg[s % 2], Boh[s % 2], gT[:, 0, at].unsqueeze(2).broadcast_to([P, BT, EQ]),
                                        ALU.mult).then_inc(S("b_ready"), 1)

                    def gated(it, s, qb=qb):
                        n = NKEY * l + qb * EQ + s + R * it
                        dve.wait_ge(S("g_mm"), n + 1)
                        at = bass.ds(it * (R * BT) + s * BT, BT)
                        g = GH[qb % 2][:, :, at].rearrange("p e t -> p t e")
                        v.tensor_tensor(g, g, bank[2 + s % 2][:, 0:BT * EQ].rearrange("p (t e) -> p t e", t=BT),
                                        ALU.mult).then_inc(S("gm_ev"), 1)

                    def body(it):
                        for s in range(R):
                            spread(it, s)
                            gated(it, s)

                    steps(dve, EQ // R, l == 0 and qb == 0, body)
                dve.wait_ge(S("acc_done"), l + 1)
                for i in range(4):
                    m = v.tensor_tensor(X[:, 2 * i:2 * i + 2, XS], X[:, 2 * i:2 * i + 2, XS],
                                        bank[4 + i][:, :].rearrange("p (a b) -> p a b", a=2), ALU.add)
                m.then_inc(S("peer_out"), 1)
                dve.wait_ge(S("peer_out"), l + 1)
            norm_out("fin", X[:, :, XS], T, k("gfin"), X[:, :, XS])

            dve.wait_ge(S("norm_out"), 5)
            seq(v.tensor_tensor(col[:, 60:62], k("lq"), k("lk"), ALU.mult))
            dve.nop().then_inc(S("lam_prod"), 1)
            dve.wait_ge(S("lam_exp"), 1)
            seq(v.tensor_tensor(nlam[:, :], col[:, 62:63], col[:, 63:64], ALU.subtract))
            seq(v.tensor_scalar(nlam[:, :], nlam[:, :], LAM_INIT, None, ALU.add))
            for a, name, scale in ((64, "daq", 0.125), (65, "mqn", 192 ** -0.5), (66, "mqr", 192 ** -0.5),
                                   (67, "naq", 0.125), (68, "dao", 1.0 - LAM_INIT)):
                seq(v.tensor_scalar(col[:, a:a + 1], k(name), scale, None, ALU.mult))

            def norm_scaled(name, base, gains, halves, width):
                j = NORMS.index(name)
                dve.wait_ge(S("norm_rt"), j + 1)
                seq(v.reciprocal(rs[:, 0:width], rt[:, 0:width]))
                for c in range(C):
                    for s_ in halves:
                        xs = slice(s_ * T, (s_ + 1) * T)
                        rsl = rs[:, xs] if len(halves) == 2 else rs[:, 0:T]
                        v.scalar_tensor_tensor(out=H[:, c, xs], in0=X[:, c, xs], scalar=gains[:, c, s_:s_ + 1], in1=rsl,
                                               op0=ALU.mult, op1=ALU.mult).then_inc(S("norm_mul"), 1)

            def group_norm(j, tiles_, width, last=True):
                dve.wait_ge(S("gn_rt"), j + 1)
                seq(v.reciprocal(grs[j % 2][:, 0:width], grt[j % 4][:, 0:width]))
                for t_, gain in tiles_:
                    m = v.scalar_tensor_tensor(out=t_, in0=t_, scalar=gain, in1=grs[j % 2][:, 0:width],
                                               op0=ALU.mult, op1=ALU.mult)
                m.then_inc(S("gn_out"), 1)

            def residual(l, m_, b, gate, count):
                for s_ in ((0, 1) if l == 0 else (1,)):
                    xs = slice(s_ * T, (s_ + 1) * T)
                    src = bank[b][:, xs] if l == 0 else bank[b][:, 0:T]
                    m = v.scalar_tensor_tensor(out=X[:, m_, xs], in0=src, scalar=modv[l][:, gate * C + m_, s_:s_ + 1],
                                               in1=X[:, m_, xs], op0=ALU.mult, op1=ALU.add)
                m.then_inc(S("res_ev"), 1)

            for l in range(L):
                b0 = SB[l]
                b1 = b0 + N_MOD
                b2 = b1 + PROJ[l]
                b3 = b2 + N_OUT
                b4 = b3 + N_FIN
                w_ = T2 if l == 0 else T
                dve.wait_ge(S("tile_done"), b1)
                seq(v.tensor_tensor(modv[l], bank[5][:, 0:2 * N_MOD].rearrange("p (a b) -> p a b", b=2),
                                    k(f"mb{l}").unsqueeze(2).broadcast_to([P, N_MOD, 2]), ALU.add))
                for dst, chunk, gname in ((gA, 1, f"gm{l}"), (gF, 4, f"gf{l}")):
                    seq(v.tensor_scalar(dst, modv[l][:, chunk * C:(chunk + 1) * C, :], 1.0, None, ALU.add))
                    seq(v.tensor_tensor(dst, dst, k(gname).unsqueeze(2).broadcast_to([P, C, 2]), ALU.mult))
                norm_scaled(f"a{l}", 32 * l, gA, (0, 1), T2)
                if l == 0:
                    gains = [col[:, 64:65]] * 4 + [k("dak")] * 4
                    for j in range(8):
                        group_norm(j, [(raw[:, j, :], gains[j])], T2)
                    group_norm(8, [(raw[:, 8 + c, :], k("mqa", c, c + 1)) for c in range(2)], T2)
                    group_norm(9, [(raw[:, 10, :], k("mkva"))], T2)
                    group_norm(10, [(raw[:, 11, :], k("mkr"))], T2)
                    for j in range(4):
                        group_norm(G_MLA + j, [(raw2[:, 2 * j, :], col[:, 65:66]), (raw2[:, 2 * j + 1, :], col[:, 66:67])], T2)
                    for j in range(4):
                        group_norm(G_MLA + 4 + j, [(raw2[:, 8 + j, :], k("mk"))], T2)
                    dve.wait_ge(S("gn_ss"), G_DA)
                    for r_, t_ in enumerate(rope_tiles):
                        dve.wait_ge(S("rope_mm"), r_ + 1)
                        v.tensor_tensor(rtmp[0], bank[r_ % 4][:, 0:T], k("sin"), ALU.mult).then_inc(S("rope_ev"), 1)
                        seq(v.tensor_tensor(rtmp[1], t_[:, XS], k("cos"), ALU.mult))
                        dve.wait_ge(S("rope_ev"), r_ + 1)
                        v.tensor_tensor(t_[:, XS], rtmp[0], rtmp[1], ALU.add).then_inc(S("rope_out"), 1)
                        dve.wait_ge(S("rope_out"), r_ + 1)
                    for n in range(33):
                        if n < 32:
                            hh, qt = n // 4, n % 4
                            nk = 2 * P if qt < 2 else T2
                            dve.wait_ge(S("u_mm"), n + 1)
                            a0 = 24 + 4 * (n % 2)
                            for i in range(2 if hh < 4 else 1):
                                m = v.tensor_reduce(col[:, a0 + i:a0 + i + 1], bank[2 * (n % 2) + i][:, 0:nk], AXX, ALU.max,
                                                    negate=True)
                            m.then_inc(S("u_mx"), 1)
                        if n >= 1:
                            g = n - 1
                            nk = 2 * P if g % 4 < 2 else T2
                            a0 = 26 + 4 * (g % 2)
                            p = Pb[g % 2]
                            dve.wait_ge(S("u_exp"), g + 1)
                            if g < 16:
                                seq(v.reciprocal(col[:, a0:a0 + 2], col[:, a0:a0 + 2]))
                                seq(v.tensor_scalar(col[:, a0 + 1:a0 + 2], col[:, a0 + 1:a0 + 2], nlam[:, :], None, ALU.mult))
                                seq(v.tensor_scalar(p[:, 1, 0:nk], p[:, 1, 0:nk], col[:, a0 + 1:a0 + 2], None, ALU.mult))
                                v.scalar_tensor_tensor(out=p[:, 0, 0:nk], in0=p[:, 0, 0:nk], scalar=col[:, a0:a0 + 1],
                                                       in1=p[:, 1, 0:nk], op0=ALU.mult, op1=ALU.subtract).then_inc(S("u_p"), 1)
                            else:
                                seq(v.reciprocal(col[:, a0:a0 + 1], col[:, a0:a0 + 1]))
                                v.tensor_scalar(p[:, 0, 0:nk], p[:, 0, 0:nk], col[:, a0:a0 + 1], None, ALU.mult)\
                                    .then_inc(S("u_p"), 1)
                    for h in range(4):
                        group_norm(G_DA + h, [(mix2[:, h, :], col[:, 68:69])], T2)
                else:
                    for j in range(8):
                        group_norm(G_NA + j, [(qN[:, j, :], col[:, 67:68])], T)
                    for j in range(8):
                        group_norm(G_NA + 8 + j, [(kN[:, j, :], k("nak"))], T2)
                    for n in range(32, 65):
                        if n < 64:
                            h, qt = (n - 32) // 2, n % 2
                            a0 = 24 + 4 * (n % 2)
                            dve.wait_ge(S("u_mm"), n + 1)
                            dve.wait_ge(S(f"bias{h % NB}"), 16 * (h // NB + 1))
                            dve.wait_ge(S("u_exp"), n - 1)
                            p, b = Pb[n % 2], bank[2 * (n % 2)]
                            v.tensor_copy(p[:, 1, 0:T], b[:, 0:T])
                            v.tensor_tensor(p[:, 1, T:], b[:, T:], nab[h % NB][:, qt, :], ALU.add).then_inc(S("u_sc"), 1)
                            dve.wait_ge(S("u_sc"), n - 31)
                            v.tensor_reduce(col[:, a0:a0 + 1], p[:, 1, :], AXX, ALU.max, negate=True).then_inc(S("u_mx"), 1)
                        if n >= 33:
                            g = n - 1
                            a0 = 26 + 4 * (g % 2)
                            dve.wait_ge(S("u_exp"), g + 1)
                            seq(v.reciprocal(col[:, a0:a0 + 1], col[:, a0:a0 + 1]))
                            v.tensor_scalar(Pb[g % 2][:, 0, :], Pb[g % 2][:, 0, :], col[:, a0:a0 + 1], None, ALU.mult)\
                                .then_inc(S("u_p"), 1)
                for m_ in range(C):
                    dve.wait_ge(S("tile_done"), b2 + m_ + 1)
                    residual(l, m_, m_ % 4, 2, m_)
                dve.wait_ge(S("res_ev"), 2 * C * l + C)
                norm_scaled(f"f{l}", 0, gF, (0, 1) if l == 0 else (1,), w_)
                for m_ in range(KF):
                    dve.wait_ge(S("tile_done"), b3 + 2 * m_ + 2)
                    dve.wait_ge(S("silu"), KF * l + m_ + 1)
                    v.tensor_tensor(hid[:, m_, 0:w_], sg[m_ % 2][:, 0:w_], bank[2 * (m_ % 2) + 1][:, 0:w_], ALU.mult)\
                        .then_inc(S("hid"), 1)
                for half in range(2):
                    dve.wait_ge(S("tile_done"), b4 + (half + 1) * (KF // 2))
                    for m_ in range(4):
                        residual(l, 4 * half + m_, 4 * (1 - half) + m_, 5, m_)
                dve.wait_ge(S("res_ev"), 2 * C * (l + 1))

        @block.gpsimd
        def _(pool):
            pool.wait_ge(S("const_in"), 16)
            for l in range(L):
                pool.wait_ge(S("op_ev"), N_OUT * (l + 1))
                pool.dma_start(keysT.rearrange("p a b -> p (a b)"), keys_d[l]).then_inc(S("keys_in"), 16)
            pool.wait_ge(S("peer_out"), L)
            pool.dma_start(mlaw.rearrange("p a b -> p (a b)"), mla_d).then_inc(S("mla_in"), 16)
            pool.wait_ge(S("res_ev"), 2 * C)
            for h in range(16):
                if h >= NB:
                    pool.wait_ge(S("u_sc"), 2 * (h - NB + 1))
                pool.dma_start(nab[h % NB].rearrange("p a b -> p (a b)"), bias_d[h]).then_inc(S(f"bias{h % NB}"), 16)


def kernel(**inputs):
    import concourse.bacc as _bacc
    from concourse.bass_utils import run_bass_kernel_spmd as _run

    i = {n: np.asarray(a) for n, a in inputs.items()}
    arrays = {
        "weights": weight_stream(i), "constants": constants(i), "keys": key_blocks(i), "mla": mla_blocks(i),
        "bias": na_bias(i), "x": np.ascontiguousarray(i["x"][0].T), "context": np.ascontiguousarray(i["ctx_2"][0].T),
    }
    nc = _bacc.Bacc("TRN2", target_bir_lowering=False, num_devices=1)
    aps = {n: nc.dram_tensor(n, a.shape, F32, kind="ExternalInput").ap() for n, a in arrays.items()}
    out = nc.dram_tensor("out", (D, T), F32, kind="ExternalOutput").ap()
    build(nc, aps["weights"], aps["constants"], aps["keys"], aps["mla"], aps["bias"], aps["x"], aps["context"], out)
    r = _run(nc, [arrays], core_ids=[0])
    return np.ascontiguousarray(r.results[0]["out"].T)[None]
```

```python
import math
from contextlib import ExitStack

import numpy as np
import concourse.bass as bass
from concourse import mybir

F32 = mybir.dt.float32
F32R = mybir.dt.float32r
U32 = mybir.dt.uint32
ALU = mybir.AluOpType
ACT = mybir.ActivationFunctionType
AXX = mybir.AxisListType.X

P = 128
D = 1024
C = D // P
T = 256
T2 = 2 * T
L = 2
HEADS, HD = 8, 64
TAPS, RTAPS = 31, 4
PH, TOPK, NKEY = 8, 16, 128
NQ = 4
EQ = NKEY // NQ
BT = T // EQ
R = 8
RAW, SPL = 4, 4
LEAD = 3
MV = 4
FF = 2816
KF = FF // P
NEG = -1e30
EPS = 1e-6
LAM_INIT = 0.2

N_IN, N_OUT, N_WQ = 20, 8, 16
N_PEER = 2 * NKEY
N1 = N_IN + N_OUT + N_WQ + N_PEER
PHASES = [("u", 0, None), ("u", 1, 0), ("v", 0, None), ("u", 2, 1), ("v", 1, None),
          ("u", 3, 2), ("v", 2, 3), ("v", 3, None)]
N_MOD = 48
N_FIN, N_FOUT = 2 * KF, KF
PROJ = [16, 24]
MOD0 = L * N1
SB = [MOD0, MOD0 + N_MOD + PROJ[0] + N_OUT + N_FIN + N_FOUT]
NTILES = SB[1] + N_MOD + PROJ[1] + N_OUT + N_FIN + N_FOUT

POOL_TILES = [(l * N1 + N_IN + N_OUT, l * N1 + N_IN + N_OUT + N_WQ + EQ) for l in range(L)] + \
             [(b + LEAD, b + LEAD + 40) for b in SB]

CONST = {}
_at = 0
for _name, _w in ([(f"{n}{l}", w) for l in range(L) for n, w in (
        ("g1_", C), ("g2_", C), ("bf", 1), ("cw", 2 * TAPS), ("cb", 2), ("lg", 2), ("lb", 2),
        ("rw", 2 * RTAPS), ("rb", 2), ("wr", 2 * P), ("wi", 2 * P), ("br", 2), ("bi", 2), ("lam", 2),
        ("wf", C * HEADS), ("mb", N_MOD), ("gm", C), ("gf", C))] +
        [("gfin", C), ("cc", 2 * C), ("daq", 1), ("dak", 1), ("lq", 2), ("lk", 2), ("dao", 1),
         ("mqa", 2), ("mkva", 1), ("mqn", 1), ("mqr", 1), ("mk", 1), ("mkr", 1), ("naq", 1), ("nak", 1),
         ("ident", P), ("ones", P), ("half", P), ("rot", P),
         ("mask", P), ("iota", P), ("cos", T), ("sin", T)]):
    CONST[_name] = (_at, _w)
    _at += _w
NCONST = _at


def cols(a):
    return np.ascontiguousarray(np.asarray(a).reshape(-1, P).T)


def tiles(w):
    k, n = w.shape
    return w.reshape(k // P, P, n // P, P).transpose(2, 1, 0, 3).reshape(n // P, P, k)


def weight_stream(i):
    out = []
    for l in range(L):
        w = i["w_in"][l]
        c0 = 3 * 512 + HEADS
        feat = np.concatenate([w[:, c0:c0 + 512], w[:, c0 + 512:c0 + 768], w[:, c0 + 768:c0 + 1024],
                               w[:, 0:512], w[:, 512:1024], w[:, 1024:1536]], 1)
        out += [tiles(feat), tiles(i["w_out"][l]), tiles(i["peer_wq"][l])]
        u = i["peer_u"][l].reshape(NKEY, NKEY, C, P).transpose(1, 3, 2, 0).reshape(NKEY, P, C * NKEY)
        v = i["peer_v"][l].reshape(NKEY, NKEY, D).transpose(1, 0, 2)
        for kind, q, _ in PHASES:
            out.append((u if kind == "u" else v)[q * EQ:(q + 1) * EQ])
    for l in range(L):
        out.append(tiles(i["mod_w_2"][l]))
        if l == 0:
            w = i["ev_w_in_2"][0]
            kr = np.pad(w[:, 1920:1984], ((0, 0), (0, 64)))
            out.append(tiles(np.concatenate([w[:, 0:1024], w[:, 1536:1920], kr, w[:, 1024:1536]], 1)))
        else:
            out.append(tiles(i["od_w_in_2"][0]))
        out.append(tiles(i["w_out_2"][l]))
        f = i["ffn_w_in_2"][l].reshape(D, 2, KF, P).transpose(0, 2, 1, 3).reshape(D, 2 * FF)
        out.append(tiles(f))
        f = i["ffn_w_out_2"][l].reshape(KF // 2, 2, P, 2, 4, P).transpose(3, 0, 2, 1, 4, 5)
        out.append(f.reshape(KF, P, D))
    return np.ascontiguousarray(np.concatenate(out, 0))


def constants(i):
    c = np.zeros((P, NCONST), np.float32)

    def put(name, a):
        at, w = CONST[name]
        a = np.asarray(a)
        c[:a.shape[0], at:at + w] = a

    def twice(a):
        return np.concatenate([a, a])[:, None]

    for l in range(L):
        put(f"g1_{l}", cols(i["norm1_g"][l]))
        put(f"g2_{l}", cols(i["norm2_g"][l]))
        put(f"bf{l}", i["b_forget"][l][:, None])
        put(f"cw{l}", i["conv_dw_w"][l].reshape(TAPS, 2, P).transpose(2, 1, 0).reshape(P, 2 * TAPS))
        put(f"cb{l}", cols(i["conv_dw_b"][l]))
        put(f"lg{l}", cols(i["conv_ln_g"][l]))
        put(f"lb{l}", cols(i["conv_ln_b"][l]))
        put(f"rw{l}", i["rg_conv_w"][l].reshape(RTAPS, 2, P).transpose(2, 1, 0).reshape(P, 2 * RTAPS))
        put(f"rb{l}", cols(i["rg_conv_b"][l]))
        for n, k in (("wr", "rg_w_r"), ("wi", "rg_w_i")):
            w = np.zeros((P, 2, P), np.float32)
            for c_ in range(2):
                for b in range(2):
                    w[64 * b:64 * b + 64, c_, 64 * b:64 * b + 64] = i[k][l][2 * c_ + b]
            put(f"{n}{l}", w.reshape(P, 2 * P))
        put(f"br{l}", cols(i["rg_b_r"][l]))
        put(f"bi{l}", cols(i["rg_b_i"][l]))
        put(f"lam{l}", cols(i["rg_lambda"][l]))
        put(f"wf{l}", i["w_in"][l][:, 1536:1544].reshape(C, P, HEADS).transpose(1, 0, 2).reshape(P, -1))
        put(f"mb{l}", cols(i["mod_b_2"][l]))
        put(f"gm{l}", cols(i["norm_mix_g_2"][l]))
        put(f"gf{l}", cols(i["norm_ffn_g_2"][l]))
    put("gfin", cols(i["final_g"]))
    put("cc", np.stack([cols(i["c_ctx_2"]), cols(i["c_2"][0])], 2).reshape(P, 2 * C))
    put("daq", twice(i["da_q_g_2"][0]))
    put("dak", twice(i["da_k_g_2"][0]))
    put("lq", np.stack([i["da_lq1_2"][0], i["da_lq2_2"][0]], 1))
    put("lk", np.stack([i["da_lk1_2"][0], i["da_lk2_2"][0]], 1))
    put("dao", i["da_out_g_2"][0][:, None])
    put("mqa", cols(i["mla_q_a_g_2"][0]))
    put("mkva", cols(i["mla_kv_a_g_2"][0]))
    put("mqn", i["mla_q_g_2"][0][:128, None])
    put("mqr", i["mla_q_g_2"][0][128:, None])
    put("mk", i["mla_k_g_2"][0][:, None])
    put("mkr", i["mla_kr_g_2"][0][:, None])
    put("naq", twice(i["na_q_g_2"][0]))
    put("nak", twice(i["na_k_g_2"][0]))
    p = np.arange(P)
    put("ident", np.eye(P))
    put("ones", np.ones((P, P)))
    put("half", (p[:, None] // 64 == p[None, :] // 64))
    rot = np.zeros((P, P))
    for m in range(P):
        rot[m + 16 if m % 32 < 16 else m - 16, m] = -1.0 if m % 32 < 16 else 1.0
    put("rot", rot)
    put("mask", np.where(p[None, :] <= p[:, None], 0.0, NEG))
    put("iota", np.tile(p[None, :], (P, 1)))
    t = np.arange(T)
    half = 32
    inv = (np.float32(10000.0) ** (-np.arange(0, half, 2, dtype=np.float32) / np.float32(half))).astype(np.float32)
    d = p % 64
    pos = np.where(d[:, None] < 32, (t // 64)[None, :], (t % 64)[None, :]).astype(np.float32)
    ang = (pos * inv[d % 16][:, None]).astype(np.float32)
    put("cos", np.cos(ang).astype(np.float32))
    put("sin", np.sin(ang).astype(np.float32))
    return c


def mla_blocks(i):
    uq = i["mla_w_uq_2"][0].reshape(2, P, 4, 192)
    uq = np.pad(uq, ((0, 0), (0, 0), (0, 0), (0, 64))).reshape(2, P, 4, 2, P)
    out = [uq[c, :, h, part] for h in range(4) for part in range(2) for c in range(2)]
    ukv = i["mla_w_ukv_2"][0].reshape(P, 4, 256)
    out += [ukv[:, h, :128] for h in range(4)] + [ukv[:, h, 128:] for h in range(4)]
    return np.ascontiguousarray(np.stack(out, 1).reshape(P, 24 * 128))


def key_blocks(i):
    k = np.stack([i["peer_k1"], i["peer_k2"]], 2)
    return np.ascontiguousarray(k.transpose(0, 4, 1, 2, 3).reshape(L, P, 2 * PH * NKEY))


def na_bias(i):
    q, k = np.arange(T), np.arange(T)
    dr = (k // 64)[None, :] - (q // 64)[:, None]
    dc = (k % 64)[None, :] - (q % 64)[:, None]
    start = np.clip(q % 64 - 8, 0, 48)
    ok = ((k % 64)[None, :] >= start[:, None]) & ((k % 64)[None, :] < start[:, None] + 16)
    b = i["na_rpb_2"][0][:, dr + 7, np.clip(dc, -15, 15) + 15]
    b = np.where(ok[None], b, np.float32(NEG)).astype(np.float32)
    return np.ascontiguousarray(b.reshape(16, 2, P, T).transpose(0, 2, 1, 3).reshape(16, P, 2 * T))


def after(eng, sem, value):
    if not isinstance(value, int) or value > 0:
        eng.wait_ge(sem, value)


def steps(eng, n, peel, body):
    if peel:
        body(0)
    with eng.Fori(1 if peel else 0, n) as it:
        body(it)


def build(nc, wts, cst_d, keys_d, mla_d, bias_d, x_d, ctx_d, out_d, stop_after=None):
    ctx = ExitStack()
    with ctx:
        def sb(name, shape, dt=F32):
            return ctx.enter_context(nc.sbuf_tensor(name, shape, dt))

        sems = {}

        def S(name):
            if name not in sems:
                sems[name] = ctx.enter_context(nc.semaphore(name))
            return sems[name]

        X = sb("X", [P, C, T2])
        ring = sb("ring", [P, RAW, 8, P])
        Wh = sb("Wh", [P, SPL, 8, P], F32R)
        Wl = sb("Wl", [P, SPL, 8, P], F32R)
        at_hr = nc.sbuf_base
        sb("HR_room", [P, 2, C, T2])
        HR = nc.alloc_sbuf_tensor_at("HR", [P, 2, C, T2], F32R, offset=at_hr)
        HA = nc.alloc_sbuf_tensor_at("HA", [P, 2 * C * T2], F32, offset=at_hr)
        Hh, Hl = HR[:, 0], HR[:, 1]
        K = sb("K", [P, NCONST])
        NAR = 25312
        arena = sb("arena", [P, NAR])
        eps = sb("eps", [P, 1])
        zero = sb("zero", [P, P])
        nlam = sb("nlam", [P, 1])
        col = sb("col", [P, 96])
        bank = [ctx.enter_context(nc.psum_tensor(f"bank{i}", [P, 512], F32)) for i in range(8)]

        XS = slice(T, T2)

        def k(name, a=0, b=None):
            at, w = CONST[name]
            return K[:, at + a:at + (w if b is None else b)]

        top = [0]

        def area(*dims, at=None):
            n = int(np.prod(dims))
            o = top[0] if at is None else at
            top[0] = o + n
            assert o + n <= NAR, (o, n)
            a = arena[:, o:o + n]
            if len(dims) == 2:
                a = a.rearrange("p (a b) -> p a b", a=dims[0])
            if len(dims) == 3:
                a = a.rearrange("p (a b c) -> p a b c", a=dims[0], b=dims[1])
            return a

        GH = [area(EQ, T, at=0), area(EQ, T, at=EQ * T)]
        top[0] = 0
        cvA, cvG, yconv, cen, sqc = (area(2, T) for _ in range(5))
        ypad, rpad = area(2, T + TAPS - 1), area(2, T + RTAPS - 1)
        gateG, xr, rg, ig, la, aa, th, m2, bx, hs = (area(2, T) for _ in range(10))
        qT, kT = area(4, T), area(4, T)
        vtok = area(2, 512)
        fz = [area(T) for _ in range(6)]
        cum, ncum = area(T), area(T)
        sel = area(HEADS, P)
        sc = [area(3 * P) for _ in range(2)]
        assert top[0] <= 16384
        top[0] = 16384
        mixT = area(C, T)
        hi0 = top[0]
        sq1 = area(C, T)
        rt, rs = area(T), area(T)
        biasT = area(HEADS, 3 * P)
        Pm = [area(3 * P) for _ in range(2)]
        PT = [arena[:, i * 3 * P:(i + 1) * 3 * P] for i in range(2)]
        cT = area(2, HEADS)
        top[0] = 16384
        keysT = area(16, P)
        assert top[0] <= hi0
        qs = [area(T) for _ in range(2)]
        w1 = area(P)
        Boh, Bg = [area(BT, EQ) for _ in range(2)], [area(BT, EQ) for _ in range(2)]
        gT = area(3, T)
        top[0] -= 4 * BT * EQ + 3 * T
        v12, i12, if12 = area(2, 16, 16), area(2, 16, 16), area(2, 16, 16)
        cand, cand2 = area(256), area(256)
        ca, cb = area(2, 8, 16), area(2, 8, 16)
        sv, ci = area(2, 8, 16), area(2, 8, 16)
        gte = area(2, 3, P)
        ssum = area(2, 8)
        oneh = area(8, 16, 16)
        top[0] -= 2 * BT * P
        Aoh = [area(BT, P) for _ in range(2)]
        i12u, ciu = i12.bitcast(U32), ci.bitcast(U32)
        cau, cbu = ca.bitcast(U32), cb.bitcast(U32)

        rt1, rs1 = rt, rs
        raw, vda = area(12, T2, at=0), area(4, 512)
        raw2, vml = area(12, T2), area(4, 512)
        sqg = [area(2, T2) for _ in range(2)]
        rtmp = [sqg[0][:, 0, i * T:(i + 1) * T] for i in range(2)]
        top[0] = hi0
        sq2 = area(C, T2)
        grt = [area(T2) for _ in range(2)]
        grs = [area(T2) for _ in range(2)]
        rt2, rs2 = grt[0], grs[0]
        modv = [area(N_MOD, 2) for _ in range(L)]
        gA, gF = area(C, 2), area(C, 2)
        cs = sb("cs", [P, 2, C, 2], F32R)
        csil, csig = area(C, 2), area(C, 2)
        mix2 = sq2
        mlaw = HA[:, 0:24 * P].rearrange("p (a b) -> p a b", b=P)
        Pb = [HA[:, 3072 + i * 1024:4096 + i * 1024].rearrange("p (a b) -> p a b", a=2) for i in range(2)]
        AT = [HA[:, 5120 + i * 512:5632 + i * 512].rearrange("p (a b) -> p a b", a=4) for i in range(2)]
        assert top[0] <= NAR
        hid, sg = area(KF, T2, at=0), [area(T2) for _ in range(2)]
        qN, kN, vN = area(C, T, at=0), area(C, T2), area(4, D)
        NB = 4
        nab = [area(2, T) for _ in range(NB)]
        assert top[0] <= hi0 - 2048
        G_MLA, G_DA, G_NA = 11, 19, 23

        OUT_RES = 4 * C
        SPLITS = {}
        _n = 0
        for name_, pieces in (("n1.0", 2), ("m0", 2), ("n2.0", 2), ("n1.1", 2), ("m1", 2), ("n2.1", 2),
                              ("a0", 16), ("m2", 4), ("f0", 16), ("a1", 16), ("m3", 2), ("f1", 8)):
            SPLITS[name_] = (_n, _n + pieces)
            _n += pieces
        MULS, _n = {}, 0
        for name_ in ("n1.0", "n2.0", "n1.1", "n2.1", "a0", "f0", "a1", "f1"):
            MULS[name_] = (_n, _n + SPLITS[name_][1] - SPLITS[name_][0])
            _n = MULS[name_][1]

        def squares_of(name):
            return sq1 if name[0] == "n" or name == "fin" else sq2

        NORMS = ["n1.0", "n2.0", "n1.1", "n2.1", "fin", "a0", "f0", "a1", "f1"]
        ident = k("ident")
        rope_tiles = [raw[:, i, :] for i in (0, 1, 2, 3, 4, 5, 6, 7, 11)] + [raw2[:, 2 * h + 1, :] for h in range(4)]
        block = ctx.enter_context(nc.Block())

        def slot_value(i, it=0):
            return 16 * (i // RAW + 1) + 16 * (R // RAW) * it

        @block.sync
        def _(sp):
            sp.dma_start(K[:], cst_d).then_inc(S("const_in"), 16)
            sp.dma_start(X[:, :, 0:T], ctx_d.rearrange("(c p) t -> p c t", p=P)).then_inc(S("ctx_in"), 16)
            sp.dma_start(X[:, :, XS], x_d.rearrange("(c p) t -> p c t", p=P)).then_inc(S("x_in"), 16)

            def load(i, slot):
                sp.dma_start(ring[:, slot].rearrange("p a b -> p (a b)"),
                             wts[bass.ds(i, 1), :, :].rearrange("o p n -> (o p) n")).then_inc(S(f"tile{slot}"), 16)

            total = NTILES if stop_after is None else stop_after
            for i in range(R):
                after(sp, S("lo_done"), i - RAW + 1)
                load(i, i % RAW)
            with sp.Fori(1, total // R) as it:
                for s in range(R):
                    sp.wait_ge(S("lo_done"), it * R + (s - RAW + 1))
                    load(it * R + s, s % RAW)
            for i in range(total // R * R, total):
                sp.wait_ge(S("lo_done"), i - RAW + 1)
                load(i, i % RAW)
            sp.wait_ge(S("res_ev"), OUT_RES)
            sp.dma_start(out_d.rearrange("(c p) t -> p c t", p=P), X[:, :, XS]).then_inc(S("out"), 16)
            sp.wait_ge(S("out"), 16)

        @block.tensor
        def _(pe):
            def mm(out, lhsT, rhs, first, last):
                return nc.tensor.matmul(out, lhsT, rhs, start=first, stop=last)

            def high(i, it=0):
                pe.wait_ge(S("hi_done"), i + 1 + R * it)
                return Wh[:, i % SPL]

            def rest(i, it=0):
                pe.wait_ge(S("lo_done"), i + 1 + R * it)
                return Wl[:, i % SPL]

            def norm_sums(name, n=T):
                j = NORMS.index(name)
                pe.wait_ge(S("norm_sq"), j + 1)
                for c in range(C):
                    m = mm(bank[7][:, 0:n], k("ones"), squares_of(name)[:, c, 0:n], c == 0, c == C - 1)
                m.then_inc(S("norm_ss"), 1)

            def feature_tile(i, out, mh, ml, it=0):
                w = high(i, it)
                for c in range(C):
                    mm(out, w[:, c, :], mh[:, c, :], c == 0, False)
                    mm(out, w[:, c, :], ml[:, c, :], False, False)
                w = rest(i, it)
                for c in range(C):
                    m = mm(out, w[:, c, :], mh[:, c, :], False, c == C - 1)
                m.then_inc(S("tile_done"), 1)

            def token_tile(i, out, tts, first):
                w = high(i)
                pe.wait_ge(S("lo_done"), i + 1)
                for tt in range(tts):
                    o, x_ = out[:, tt * P:(tt + 1) * P], slice(first + tt * P, first + (tt + 1) * P)
                    for c in range(C):
                        mm(o, Hh[:, c, x_], w[:, c, :], c == 0, False)
                        mm(o, Hl[:, c, x_], w[:, c, :], False, False)
                        m = mm(o, Hh[:, c, x_], Wl[:, i % SPL, c, :], False, c == C - 1)
                m.then_inc(S("tile_done"), 1)

            Hx = (Hh[:, :, XS], Hl[:, :, XS])
            Hw = (Hh, Hl)
            pe.wait_ge(S("const_in"), 16)
            for l in range(L):
                t0 = l * N1
                norm_sums(f"n1.{l}")
                pe.wait_ge(S("h_mul"), MULS[f"n1.{l}"][1])
                for c in range(C):
                    m = mm(bank[4][0:HEADS, 0:T], k(f"wf{l}", c * HEADS, (c + 1) * HEADS), sq1[:, c, :], c == 0, c == C - 1)
                m.then_inc(S("f_mm"), 1)
                pe.wait_ge(S("h_out"), SPLITS[f"n1.{l}"][1])
                for m_ in range(16):
                    if m_ >= 4:
                        pe.wait_ge(S("proj_ev"), N_IN * l + m_ - 3)
                    feature_tile(t0 + m_, bank[m_ % 4][:, 0:T], *Hx)
                    if m_ == 11:
                        pe.wait_ge(S("xr_ready"), l + 1)
                        for g, wname in ((0, "wr"), (1, "wi")):
                            for c in range(2):
                                m = mm(bank[5 + g][:, c * T:(c + 1) * T], k(f"{wname}{l}", c * P, (c + 1) * P),
                                       xr[:, c, :], True, True)
                        m.then_inc(S("rg_mm"), 1)
                for n in range(4):
                    pe.wait_ge(S("proj_ev"), N_IN * l + 16 + n - 3)
                    token_tile(t0 + 16 + n, bank[n], 2, T)
                pe.wait_ge(S("cum_ready"), l + 1)
                pe.wait_ge(S("proj_ev"), N_IN * (l + 1))
                pe.wait_ge(S("rg_ev"), 2 * l + 2)
                for tt in range(2):
                    mm(bank[5][:, tt * HEADS:(tt + 1) * HEADS], cum[0:HEADS, tt * P:(tt + 1) * P],
                       ident[0:HEADS, 0:HEADS], True, True)
                for h in range(HEADS):
                    m = mm(bank[(0, 1, 2, 4)[h // 2]][:, (h % 2) * T:(h % 2 + 1) * T], sel[0:HEADS, h, :],
                           ncum[0:HEADS, :], True, True)
                m.then_inc(S("bc_mm"), 1)
                pe.wait_ge(S("bc_ev"), l + 1)
                def head_scores(h):
                    po, hc, b = slice(64 * (h % 2), 64 * (h % 2) + 64), h // 2, bank[4 + h % 2]
                    if h >= 2:
                        pe.wait_ge(S("att_sc"), HEADS * l + h - 1)
                    mm(b[:, 0:P], qT[po, hc, 0:P], kT[po, hc, 0:P], True, True)
                    mm(b[:, P:3 * P], qT[po, hc, P:T], kT[po, hc, :], True, True).then_inc(S("att_mm"), 1)

                head_scores(0)
                for h in range(HEADS + 2):
                    if h + 1 < HEADS:
                        head_scores(h + 1)
                    if h >= 2:
                        g = h - 2
                        po, hc = slice(64 * (g % 2), 64 * (g % 2) + 64), g // 2
                        pe.wait_ge(S("pt_ev"), HEADS * l + g + 1)
                        if hc >= 2:
                            pe.wait_ge(S("y_ev"), 4 * l + hc - 1)
                        yb = bank[hc % 2]
                        mm(yb[po, 0:T], vtok[:, 0, g * HD:(g + 1) * HD], PT[g % 2][:, 0:T], True, False)
                        mm(yb[po, P:T], vtok[:, 1, g * HD:(g + 1) * HD], PT[g % 2][:, T:3 * P], False, True)\
                            .then_inc(S("pv_mm"), 1)
                    if 1 <= h <= HEADS:
                        g = h - 1
                        pe.wait_ge(S("p_ready"), HEADS * l + g + 1)
                        if g >= 2:
                            pe.wait_ge(S("pt_ev"), HEADS * l + g - 1)
                        for i in range(3):
                            m = nc.tensor.transpose(bank[6 + g % 2][:, i * P:(i + 1) * P], Pm[g % 2][:, i * P:(i + 1) * P], ident)
                        m.then_inc(S("pt_mm"), 1)
                pe.wait_ge(S("conv_done"), l + 1)
                for c in range(2):
                    m = mm(bank[3][:, 0:T], k("ones"), yconv[:, c, :], c == 0, c == 1)
                m.then_inc(S("ln_sum"), 1)
                pe.wait_ge(S("ln_sq"), l + 1)
                for c in range(2):
                    m = mm(bank[3][:, 0:T], k("ones"), sqc[:, c, :], c == 0, c == 1)
                m.then_inc(S("ln_var"), 1)
                pe.wait_ge(S("y_ev"), 4 * (l + 1))
                pe.wait_ge(S("ln_out"), 2 * (l + 1))
                pe.wait_ge(S("rnn_out"), l + 1)
                pe.wait_ge(S("h_out"), SPLITS[f"m{l}"][1])
                for m_ in range(N_OUT):
                    if m_ >= 4:
                        pe.wait_ge(S("op_ev"), N_OUT * l + m_ - 3)
                    feature_tile(t0 + N_IN + m_, bank[m_ % 4][:, 0:T], *Hx)
                norm_sums(f"n2.{l}")
                pe.wait_ge(S("h_out"), SPLITS[f"n2.{l}"][1])
                pe.wait_ge(S("keys_in"), 16 * (l + 1))
                for j in range(N_WQ + 1):
                    if j < N_WQ:
                        if j >= 2:
                            pe.wait_ge(S("qs_ev"), N_WQ * l + j - 1)
                        feature_tile(t0 + N_IN + N_OUT + j, bank[j % 2][:, 0:T], *Hx)
                    if j >= 1:
                        i = j - 1
                        pe.wait_ge(S("qs_ev"), N_WQ * l + i + 1)
                        if i >= 2:
                            pe.wait_ge(S("top_ev"), N_WQ * l + i - 1)
                        for tt in range(2):
                            m = mm(bank[2 + i % 2][:, tt * P:(tt + 1) * P], qs[i % 2][:, tt * P:(tt + 1) * P],
                                   keysT[:, i, :], True, True)
                        m.then_inc(S("s_mm"), 1)
                p0 = t0 + N_IN + N_OUT + N_WQ
                for i in range(4):
                    mm(bank[4 + i][:, :], zero[:, :], K[:, 0:512], True, False)
                for pi, (kind, q, qb) in enumerate(PHASES):
                    base = p0 + pi * EQ
                    if pi == 1:
                        for tt in range(2):
                            pe.wait_ge(S("gate_ready"), 2 * l + tt + 1)
                            for i in range(3):
                                m = nc.tensor.transpose(bank[2 + tt][:, i * P:(i + 1) * P], gte[:, tt, i, :], ident)
                            m.then_inc(S("gt_mm"), 1)
                        pe.wait_ge(S("gt_ev"), 2 * (l + 1))

                    def body(it, kind=kind, q=q, qb=qb, base=base):
                        for s in range(R):
                            if kind == "u":
                                pe.wait_ge(S("h_ev"), NKEY * l + q * EQ + s + 1 + R * it)
                                feature_tile(base + s, bank[s % 2][:, 0:T], *Hx, it)
                            else:
                                gh, gl = Hh[:, s % MV, 0:T], Hl[:, s % MV, 0:T]
                                w = high(base + s, it)
                                pe.wait_ge(S("mv_lo"), NKEY * l + q * EQ + s + 1 + R * it)
                                for m_ in range(C):
                                    o = bank[4 + m_ // 2][:, (m_ % 2) * T:(m_ % 2 + 1) * T]
                                    mm(o, w[:, m_, :], gh, False, False)
                                    mm(o, w[:, m_, :], gl, False, False)
                                w = rest(base + s, it)
                                for m_ in range(C):
                                    m = mm(bank[4 + m_ // 2][:, (m_ % 2) * T:(m_ % 2 + 1) * T], w[:, m_, :], gh, False, False)
                                m.then_inc(S("tile_done"), 1)
                            if qb is not None:
                                n = NKEY * l + qb * EQ + s + R * it
                                pe.wait_ge(S("a_ready"), n + 1)
                                pe.wait_ge(S("b_ready"), n + 1)
                                after(pe, S("gm_ev"), n - 1)
                                for i in range(BT):
                                    m = mm(bank[2 + s % 2][:, i * EQ:(i + 1) * EQ], Aoh[s % 2][:, i, :],
                                           Bg[s % 2][:, i, :], True, True)
                                m.then_inc(S("g_mm"), 1)

                    steps(pe, EQ // R, l == 0 and pi == 1, body)
                for i in range(4):
                    m = mm(bank[4 + i][:, :], zero[:, :], K[:, 0:512], False, True)
                m.then_inc(S("acc_done"), 1)
            norm_sums("fin")

            def group_sum(j, srcs, ones_, width):
                pe.wait_ge(S("gn_sq"), j + 1)
                if j >= 4:
                    pe.wait_ge(S("gn_rt"), j - 3)
                for n in range(srcs):
                    m = mm(bank[4 + j % 4][:, 0:width], ones_, sqg[j % 2][:, n, 0:width], n == 0, n == srcs - 1)
                m.then_inc(S("gn_ss"), 1)

            def transpose_unit(n, nk):
                pe.wait_ge(S("u_p"), n + 1)
                if n >= 2:
                    pe.wait_ge(S("u_ptev"), n - 1)
                for i in range(nk):
                    m = nc.tensor.transpose(bank[4 + n % 2][:, i * P:(i + 1) * P], Pb[n % 2][:, 0, i * P:(i + 1) * P], ident)
                m.then_inc(S("u_pt"), 1)

            def apply_unit(n, nk, oslice, vals):
                pe.wait_ge(S("u_ptev"), n + 1)
                for i in range(nk):
                    m = mm(oslice, vals(i), AT[n % 2][:, i, :], i == 0, i == nk - 1)
                m.then_inc(S("u_pv"), 1)

            pe.wait_ge(S("lam_prod"), 1)
            mm(bank[6][:, 0:2], k("ones"), col[:, 60:62], True, True).then_inc(S("lam_mm"), 1)
            for l in range(L):
                b0 = SB[l]
                b1 = b0 + N_MOD
                b2 = b1 + PROJ[l]
                b3 = b2 + N_OUT
                b4 = b3 + N_FIN
                xs = slice(0, T2) if l == 0 else XS
                w_ = T2 if l == 0 else T
                pe.wait_ge(S("cs_split"), 1)
                if l == 1:
                    pe.wait_ge(S("res_ev"), 2 * C)

                def mod_body(it):
                    for s in range(R):
                        o = bank[5][:, bass.ds(it * (2 * R) + 2 * s, 2)]
                        w = high(b0 + s, it)
                        for c in range(C):
                            mm(o, w[:, c, :], cs[:, 0, c, :], c == 0, False)
                            mm(o, w[:, c, :], cs[:, 1, c, :], False, False)
                        w = rest(b0 + s, it)
                        for c in range(C):
                            m = mm(o, w[:, c, :], cs[:, 0, c, :], False, c == C - 1)
                        m.then_inc(S("tile_done"), 1)

                steps(pe, N_MOD // R, False, mod_body)
                norm_sums(f"a{l}", T2)
                pe.wait_ge(S("h_out"), SPLITS[f"a{l}"][1])
                if l == 0:
                    for i in range(16):
                        if i >= 4:
                            pe.wait_ge(S("pj_ev"), i - 3)
                        if i < 12:
                            feature_tile(b1 + i, bank[i % 4][:, :], *Hw)
                        else:
                            token_tile(b1 + i, bank[i % 4], 4, 0)
                        j = i - 3
                        if 0 <= j < 11:
                            group_sum(j, 2 if j == 8 else 1, k("half") if j < 8 else k("ones"), T2)
                    pe.wait_ge(S("mla_in"), 16)
                    pe.wait_ge(S("gn_out"), 11)
                    for o in range(16):
                        pe.wait_ge(S("pj_ev"), 16 + o - 3)
                        if o < 8:
                            for c in range(2):
                                m = mm(bank[o % 4][:, :], mlaw[:, 2 * o + c, :], raw[:, 8 + c, :], c == 0, c == 1)
                        elif o < 12:
                            m = mm(bank[o % 4][:, :], mlaw[:, 8 + o, :], raw[:, 10, :], True, True)
                        else:
                            for tt in range(4):
                                m = mm(bank[o % 4][:, tt * P:(tt + 1) * P], raw[:, 10, tt * P:(tt + 1) * P],
                                       mlaw[:, 8 + o, :], True, True)
                        m.then_inc(S("p2_mm"), 1)
                    for j in range(8):
                        group_sum(G_MLA + j, 2 if j < 4 else 1, k("ones"), T2)
                    pe.wait_ge(S("pj_ev"), 32)
                    pe.wait_ge(S("gn_out"), G_DA)
                    for r_, t_ in enumerate(rope_tiles):
                        if r_ >= 4:
                            pe.wait_ge(S("rope_ev"), r_ - 3)
                        mm(bank[r_ % 4][:, 0:T], k("rot"), t_[:, XS], True, True).then_inc(S("rope_mm"), 1)
                    pe.wait_ge(S("rope_out"), len(rope_tiles))
                    def scores(n):
                        hh, qt = n // 4, n % 4
                        nk = 2 * P if qt < 2 else T2
                        qsl = slice(qt * P, (qt + 1) * P)
                        if n >= 2:
                            pe.wait_ge(S("u_exp"), n - 1)
                        sb_ = 2 * (n % 2)
                        if hh < 4:
                            for i in range(2):
                                po = slice(64 * i, 64 * i + 64)
                                m = mm(bank[sb_ + i][:, 0:nk], raw[po, hh, qsl], raw[po, 4 + hh, 0:nk], True, True)
                        else:
                            h = hh - 4
                            mm(bank[sb_][:, 0:nk], raw2[:, 2 * h, qsl], raw2[:, 8 + h, 0:nk], True, False)
                            m = mm(bank[sb_][:, 0:nk], raw2[:, 2 * h + 1, qsl], raw[:, 11, 0:nk], False, True)
                        m.then_inc(S("u_mm"), 1)

                    scores(0)
                    for n in range(34):
                        if n + 1 < 32:
                            scores(n + 1)
                        if n >= 2:
                            g = n - 2
                            hh, qt = g // 4, g % 4
                            if hh >= 2 and qt == 0:
                                pe.wait_ge(S("o_ev"), hh - 1)
                            vals = vda if hh < 4 else vml
                            apply_unit(g, 2 if qt < 2 else 4, bank[6 + hh % 2][:, qt * P:(qt + 1) * P],
                                       lambda i, vals=vals, h=hh % 4: vals[:, i, h * P:(h + 1) * P])
                        if 1 <= n <= 32:
                            transpose_unit(n - 1, 2 if (n - 1) % 4 < 2 else 4)
                    pe.wait_ge(S("o_ev"), 8)
                    for h in range(4):
                        group_sum(G_DA + h, 1, k("ones"), T2)
                    pe.wait_ge(S("gn_out"), G_NA)
                else:
                    for i in range(24):
                        if i >= 4:
                            pe.wait_ge(S("pj_ev"), 32 + i - 3)
                        if i < 8:
                            feature_tile(b1 + i, bank[i % 4][:, 0:T], *Hx)
                        elif i < 16:
                            feature_tile(b1 + i, bank[i % 4][:, :], *Hw)
                        else:
                            token_tile(b1 + i, bank[i % 4], 4, 0)
                        j = i - 3
                        if 0 <= j < 16:
                            group_sum(G_NA + j, 1, k("half"), T if j < 8 else T2)
                    pe.wait_ge(S("gn_out"), G_NA + 16)
                    pe.wait_ge(S("pj_ev"), 32 + 24)
                    def scores(n):
                        h, qt = (n - 32) // 2, n % 2
                        po = slice(64 * (h % 2), 64 * (h % 2) + 64)
                        if n >= 34:
                            pe.wait_ge(S("u_sc"), n - 32 - 1)
                        mm(bank[2 * (n % 2)][:, :], qN[po, h // 2, qt * P:(qt + 1) * P], kN[po, h // 2, :], True, True)\
                            .then_inc(S("u_mm"), 1)

                    scores(32)
                    for n in range(32, 66):
                        if n + 1 < 64:
                            scores(n + 1)
                        if n >= 34:
                            g = n - 2
                            h, qt = (g - 32) // 2, g % 2
                            hc = h // 2
                            po = slice(64 * (h % 2), 64 * (h % 2) + 64)
                            if hc >= 2 and h % 2 == 0 and qt == 0:
                                pe.wait_ge(S("o_ev"), 8 + hc - 1)
                            apply_unit(g, 4, bank[6 + hc % 2][po, qt * P:(qt + 1) * P],
                                       lambda i, h=h: vN[:, i, h * HD:(h + 1) * HD])
                        if 33 <= n <= 64:
                            transpose_unit(n - 1, 4)
                    pe.wait_ge(S("o_ev"), 16)
                Hf = (Hh[:, :, xs], Hl[:, :, xs])
                pe.wait_ge(S("h_out"), SPLITS[f"m{2 + l}"][1])
                for m_ in range(C):
                    if m_ >= 4:
                        pe.wait_ge(S("res_ev"), 2 * C * l + m_ - 3)
                    feature_tile(b2 + m_, bank[m_ % 4][:, 0:w_], *Hf)
                norm_sums(f"f{l}", w_)
                pe.wait_ge(S("h_out"), SPLITS[f"f{l}"][1])
                for m_ in range(KF):
                    if m_ >= 2:
                        pe.wait_ge(S("hid"), KF * l + m_ - 1)
                    for g in range(2):
                        feature_tile(b3 + 2 * m_ + g, bank[2 * (m_ % 2) + g][:, 0:w_], *Hf)
                pe.wait_ge(S("hid"), KF * (l + 1))
                for half in range(2):
                    for j in range(KF // 2):
                        n = half * (KF // 2) + j
                        w = high(b4 + n)
                        pe.wait_ge(S("mv_lo"), L * NKEY + KF * l + n + 1)
                        for kk in range(2):
                            for m_ in range(4):
                                o, b = bank[4 * (1 - half) + m_][:, 0:w_], 2 * (n % MV) + kk
                                mm(o, w[:, 4 * kk + m_, :], Hh[:, b, 0:w_], j == 0 and kk == 0, False)
                                mm(o, w[:, 4 * kk + m_, :], Hl[:, b, 0:w_], False, False)
                        w = rest(b4 + n)
                        for kk in range(2):
                            for m_ in range(4):
                                m = mm(bank[4 * (1 - half) + m_][:, 0:w_], w[:, 4 * kk + m_, :], Hh[:, 2 * (n % MV) + kk, 0:w_],
                                       False, j == KF // 2 - 1 and kk == 1)
                        m.then_inc(S("tile_done"), 1)

        @block.scalar
        def _(act):
            def norm_act(name, x, width, sems_):
                j = NORMS.index(name)
                for s_, v_ in sems_:
                    act.wait_ge(s_, v_)
                nc.scalar.activation(squares_of(name)[:, :, 0:width], x, ACT.Square).then_inc(S("norm_sq"), 1)
                act.wait_ge(S("norm_ss"), j + 1)
                nc.scalar.activation((rt if name[0] in "n" or name == "fin" else rt2)[:, 0:width], bank[7][:, 0:width], ACT.Sqrt, bias=eps[:, :],
                                     scale=1.0 / D).then_inc(S("norm_rt"), 1)

            hi_next = [0]

            def hi(upto, it=0):
                while hi_next[0] <= min(upto, (NTILES if stop_after is None else stop_after) - 1):
                    i = hi_next[0]
                    act.wait_ge(S(f"tile{i % RAW}"), slot_value(i, it))
                    after(act, S("tile_done"), i - SPL + 1 + R * it)
                    nc.scalar.copy(Wh[:, i % SPL], ring[:, i % RAW]).then_inc(S("hi_done"), 1)
                    hi_next[0] += 1

            def split_high(name, srcs):
                for n, (o, x_) in enumerate(srcs):
                    if name[0] != "m":
                        act.wait_ge(S("h_mul"), MULS[name][0] + n + 1)
                    nc.scalar.copy(o, x_).then_inc(S("h_hi"), 1)

            act.wait_ge(S("setup"), 1)
            hi(LEAD - 1)
            for _i in range(2):
                nc.scalar.copy(col[:, 90 + _i:91 + _i], eps[:, :]).then_inc(S("h_ev"), 1)
            for l in range(L):
                norm_act(f"n1.{l}", X[:, :, XS], T,
                         [(S("x_in"), 16)] if l == 0 else [(S("peer_out"), l)])
                split_high(f"n1.{l}", [(Hh[:, c:c + 4, XS], sq1[:, c:c + 4, :]) for c in (0, 4)])
                act.wait_ge(S("fz_ready"), l + 1)
                nc.scalar.activation(fz[1][0:HEADS, :], fz[2][0:HEADS, :], ACT.Exp, scale=-1.0).then_inc(S("fexp"), 1)
                act.wait_ge(S("lam_abs"), l + 1)
                nc.scalar.activation(col[:, 2:4], col[:, 0:2], ACT.Exp, scale=-1.0).then_inc(S("lamexp"), 1)

                def evac(i, out, src, func=ACT.Copy, scale=1.0):
                    act.wait_ge(S("tile_done"), l * N1 + i + 1)
                    nc.scalar.activation(out, src, func, scale=scale).then_inc(S("proj_ev"), 1)
                    hi(l * N1 + i + LEAD)

                for i in range(16):
                    b = bank[i % 4][:, 0:T]
                    if i < 2:
                        evac(i, cvA[:, i, :], b)
                    elif i < 4:
                        evac(i, cvG[:, i - 2, :], b, ACT.Sigmoid)
                    elif i < 6:
                        if i == 4:
                            act.wait_ge(S("pads"), l + 1)
                        evac(i, rpad[:, i - 4, RTAPS - 1:], b)
                    elif i < 8:
                        evac(i, gateG[:, i - 6, :], b, ACT.Gelu_apprx_tanh)
                    elif i < 12:
                        evac(i, qT[:, i - 8, :], b, scale=0.125)
                    else:
                        evac(i, kT[:, i - 12, :], b)
                    if i == 11:
                        act.wait_ge(S("rg_mm"), l + 1)
                        for c in range(2):
                            nc.scalar.activation(rg[:, c, :], bank[5][:, c * T:(c + 1) * T], ACT.Sigmoid,
                                                 bias=k(f"br{l}", c, c + 1))
                            m = nc.scalar.activation(ig[:, c, :], bank[6][:, c * T:(c + 1) * T], ACT.Sigmoid,
                                                     bias=k(f"bi{l}", c, c + 1))
                            m.then_inc(S("rg_ev"), 1)
                for n in range(4):
                    evac(16 + n, vtok[:, :, n * P:(n + 1) * P],
                         bank[n][:, 0:T].rearrange("p (a b) -> p a b", a=2))
                act.wait_ge(S("loga"), l + 1)
                nc.scalar.activation(aa[:, :, :], la[:, :, :], ACT.Exp).then_inc(S("rnn_exp"), 1)
                nc.scalar.activation(th[:, :, :], la[:, :, :], ACT.Tanh, scale=-1.0).then_inc(S("rnn_exp"), 1)
                act.wait_ge(S("m2_ready"), l + 1)
                nc.scalar.activation(m2[:, :, :], m2[:, :, :], ACT.Sqrt).then_inc(S("rnn_root"), 1)
                for h in range(HEADS + 2):
                    if h < HEADS:
                        act.wait_ge(S("att_mx"), HEADS * l + h + 1)
                        if h >= 2:
                            act.wait_ge(S("pt_mm"), HEADS * l + h - 1)
                        nm = col[:, 8 + 2 * (h % 2):10 + 2 * (h % 2)]
                        sm = col[:, 12 + 2 * (h % 2):14 + 2 * (h % 2)]
                        nc.scalar.activation(Pm[h % 2][:, 0:P], sc[h % 2][:, 0:P], ACT.Exp, bias=nm[:, 0:1],
                                             accum_out=sm[:, 0:1])
                        nc.scalar.activation(Pm[h % 2][:, P:], sc[h % 2][:, P:], ACT.Exp, bias=nm[:, 1:2],
                                             accum_out=sm[:, 1:2]).then_inc(S("att_exp"), 1)
                    if 1 <= h <= HEADS:
                        g = h - 1
                        act.wait_ge(S("pt_mm"), HEADS * l + g + 1)
                        if g >= 2:
                            act.wait_ge(S("pv_mm"), HEADS * l + g - 1)
                        nc.scalar.copy(PT[g % 2][:, :], bank[6 + g % 2][:, 0:3 * P]).then_inc(S("pt_ev"), 1)
                    if h >= 2:
                        g = h - 2
                        if g % 2:
                            act.wait_ge(S("pv_mm"), HEADS * l + g + 1)
                            nc.scalar.copy(mixT[:, g // 2, :], bank[(g // 2) % 2][:, 0:T]).then_inc(S("y_ev"), 1)
                act.wait_ge(S("ln_cen"), l + 1)
                nc.scalar.activation(sqc[:, :, :], cen[:, :, :], ACT.Square).then_inc(S("ln_sq"), 1)
                act.wait_ge(S("ln_var"), l + 1)
                nc.scalar.activation(rt[:, 0:T], bank[3][:, 0:T], ACT.Sqrt, bias=eps[:, :], scale=1.0 / 256)\
                    .then_inc(S("ln_root"), 1)
                act.wait_ge(S("ln_z"), l + 1)
                for c in range(2):
                    nc.scalar.activation(mixT[:, 4 + c, :], cen[:, c, :], ACT.Silu, bias=k(f"lb{l}", c, c + 1))\
                        .then_inc(S("ln_out"), 1)
                act.wait_ge(S("rnn_out"), l + 1)
                act.wait_ge(S("y_ev"), 4 * (l + 1))
                act.wait_ge(S("ln_out"), 2 * (l + 1))
                split_high(f"m{l}", [(Hh[:, c:c + 4, XS], mixT[:, c:c + 4, :]) for c in (0, 4)])
                for m_ in range(N_OUT):
                    act.wait_ge(S("tile_done"), l * N1 + N_IN + m_ + 1)
                    hi(l * N1 + N_IN + m_ + LEAD)
                norm_act(f"n2.{l}", X[:, :, XS], T, [(S("op_ev"), N_OUT * (l + 1))])
                split_high(f"n2.{l}", [(Hh[:, c:c + 4, XS], sq1[:, c:c + 4, :]) for c in (0, 4)])
                for j in range(N_WQ):
                    act.wait_ge(S("tile_done"), l * N1 + N_IN + N_OUT + j + 1)
                    if j >= 2:
                        act.wait_ge(S("s_mm"), N_WQ * l + j - 1)
                    if j == 0:
                        act.wait_ge(S("h_out"), SPLITS[f"n2.{l}"][1])
                    nc.scalar.copy(qs[j % 2][:, :], bank[j % 2][:, 0:T]).then_inc(S("qs_ev"), 1)
                    hi(l * N1 + N_IN + N_OUT + j + LEAD)
                p0 = l * N1 + N_IN + N_OUT + N_WQ
                for pi, (kind, q, qb) in enumerate(PHASES):
                    if pi == 1:
                        for tt in range(2):
                            act.wait_ge(S("sv_sub"), 2 * l + tt + 1)
                            nc.scalar.activation(gte[:, tt, 0, :], sv[:, tt, :, :].rearrange("p a b -> p (a b)"), ACT.Exp)\
                                .then_inc(S("sv_exp"), 1)
                    base = p0 + pi * EQ
                    if kind == "v":
                        act.wait_ge(S("gm_ev"), NKEY * l + (q + 1) * EQ)

                        def body(it, q=q, base=base):
                            for s in range(R):
                                n = NKEY * l + q * EQ + s + R * it
                                act.wait_ge(S("tile_done"), base + s - MV + 1 + R * it)
                                act.wait_ge(S("setup"), 1)
                                nc.scalar.copy(Hh[:, s % MV, 0:T], GH[q % 2][:, bass.ds(it * R + s, 1), :]
                                               .rearrange("p o t -> p (o t)")).then_inc(S("mv_hi"), 1)
                                hi_next[0] = base + s + LEAD
                                hi(base + s + LEAD, it)

                        steps(act, EQ // R, False, body)
                        hi_next[0] = base + EQ + LEAD
                        continue
                    if q >= 2:
                        act.wait_ge(S("tile_done"), p0 + (PHASES.index(("v", q - 2, None)) + 1) * EQ)

                    def body(it, q=q, base=base):
                        for s in range(R):
                            act.wait_ge(S("tile_done"), base + s + 1 + R * it)
                            act.wait_ge(S("const_in"), 16)
                            o = GH[q % 2][:, bass.ds(it * R + s, 1), :].rearrange("p o t -> p (o t)")
                            nc.scalar.activation(o, bank[s % 2][:, 0:T], ACT.Gelu_apprx_tanh).then_inc(S("h_ev"), 1)
                            hi_next[0] = base + s + LEAD
                            hi(base + s + LEAD, it)

                    steps(act, EQ // R, False, body)
                    hi_next[0] = base + EQ + LEAD
            norm_act("fin", X[:, :, XS], T, [(S("peer_out"), L)])

            nc.scalar.activation(csil, k("cc").rearrange("p (a b) -> p a b", a=C), ACT.Silu).then_inc(S("csil"), 1)
            act.wait_ge(S("csil"), 1)
            nc.scalar.copy(cs[:, 0], csil).then_inc(S("csil"), 1)
            act.wait_ge(S("lam_mm"), 1)
            nc.scalar.activation(col[:, 62:64], bank[6][:, 0:2], ACT.Exp).then_inc(S("lam_exp"), 1)

            def squares(j, srcs, width, bufs=2):
                if j >= 2:
                    act.wait_ge(S("gn_ss"), j - 1)
                for n, s_ in enumerate(srcs):
                    m = nc.scalar.activation(sqg[j % 2][:, n, 0:width], s_, ACT.Square)
                m.then_inc(S("gn_sq"), 1)

            def group_root(j, count, width):
                act.wait_ge(S("gn_ss"), j + 1)
                if j >= 2:
                    act.wait_ge(S("gn_out"), j - 1)
                nc.scalar.activation(grt[j % 2][:, 0:width], bank[4 + j % 4][:, 0:width], ACT.Sqrt, bias=eps[:, :],
                                     scale=1.0 / count).then_inc(S("gn_rt"), 1)

            def unit_out(n, nk):
                act.wait_ge(S("u_pt"), n + 1)
                if n >= 2:
                    act.wait_ge(S("u_pv"), n - 1)
                nc.scalar.copy(AT[n % 2][:, 0:nk, :], bank[4 + n % 2][:, 0:nk * P].rearrange("p (a b) -> p a b", b=P))\
                    .then_inc(S("u_ptev"), 1)

            def norm_shift(l, name, halves, sh):
                n = MULS[name][0]
                for c in range(C):
                    for s_ in halves:
                        n += 1
                        act.wait_ge(S("h_mul"), n)
                        xs = slice(s_ * T, (s_ + 1) * T)
                        nc.scalar.activation(Hh[:, c, xs], sq2[:, c, xs], ACT.Identity, bias=modv[l][:, sh * C + c, s_:s_ + 1])\
                            .then_inc(S("h_hi"), 1)

            for l in range(L):
                b0 = SB[l]
                b1 = b0 + N_MOD
                b2 = b1 + PROJ[l]
                b3 = b2 + N_OUT
                w_ = T2 if l == 0 else T
                xs = slice(0, T2) if l == 0 else XS
                for s in range(N_MOD):
                    act.wait_ge(S("tile_done"), b0 + s + 1)
                    hi(b0 + s + LEAD)
                norm_act(f"a{l}", X[:, :, :], T2, [(S("ctx_in"), 16), (S("norm_out"), 1)] if l == 0 else [(S("res_ev"), 2 * C)])
                norm_shift(l, f"a{l}", (0, 1), 0)
                if l == 0:
                    srcs = [[raw[:, i, :]] for i in range(8)] + [[raw[:, 8, :], raw[:, 9, :]], [raw[:, 10, :]], [raw[:, 11, :]]]
                    counts = [64] * 8 + [256, 128, 64]
                    for i in range(16):
                        act.wait_ge(S("tile_done"), b1 + i + 1)
                        if i < 12:
                            nc.scalar.copy(raw[:, i, :], bank[i % 4][:, :]).then_inc(S("pj_ev"), 1)
                        else:
                            nc.scalar.copy(vda[:, :, (i - 12) * P:(i - 11) * P],
                                           bank[i % 4][:, :].rearrange("p (a b) -> p a b", a=4)).then_inc(S("pj_ev"), 1)
                        if 1 <= i < 12:
                            act.wait_ge(S("pj_ev"), i + 1)
                            squares(i - 1, srcs[i - 1], T2)
                        if 0 <= i - 3 < 11:
                            group_root(i - 3, counts[i - 3], T2)
                        hi(b1 + i + LEAD)
                    for o in range(16):
                        act.wait_ge(S("p2_mm"), o + 1)
                        if o < 12:
                            nc.scalar.copy(raw2[:, o, :], bank[o % 4][:, :]).then_inc(S("pj_ev"), 1)
                        else:
                            nc.scalar.copy(vml[:, :, (o - 12) * P:(o - 11) * P],
                                           bank[o % 4][:, :].rearrange("p (a b) -> p a b", a=4)).then_inc(S("pj_ev"), 1)
                    act.wait_ge(S("pj_ev"), 32)
                    for j in range(9):
                        if j < 8:
                            squares(G_MLA + j, [raw2[:, 2 * j, :], raw2[:, 2 * j + 1, :]] if j < 4 else [raw2[:, 4 + j, :]], T2)
                        if j >= 1:
                            group_root(G_MLA + j - 1, 192 if j - 1 < 4 else 128, T2)
                    for n in range(34):
                        if n < 32:
                            hh, qt = n // 4, n % 4
                            nk = 2 * P if qt < 2 else T2
                            act.wait_ge(S("u_mx"), n + 1)
                            if n >= 2:
                                act.wait_ge(S("u_pt"), n - 1)
                            a0 = 24 + 4 * (n % 2)
                            for i in range(2 if hh < 4 else 1):
                                m = nc.scalar.activation(Pb[n % 2][:, i, 0:nk], bank[2 * (n % 2) + i][:, 0:nk], ACT.Exp,
                                                         bias=col[:, a0 + i:a0 + i + 1],
                                                         accum_out=col[:, a0 + 2 + i:a0 + 3 + i])
                            m.then_inc(S("u_exp"), 1)
                        if 1 <= n <= 32:
                            unit_out(n - 1, 2 if (n - 1) % 4 < 2 else 4)
                        if n >= 2:
                            g = n - 2
                            if g % 4 == 3:
                                act.wait_ge(S("u_pv"), g + 1)
                                nc.scalar.copy(mix2[:, g // 4, :], bank[6 + (g // 4) % 2][:, :]).then_inc(S("o_ev"), 1)
                    act.wait_ge(S("o_ev"), 8)
                    for j in range(5):
                        if j < 4:
                            squares(G_DA + j, [mix2[:, j, :]], T2)
                        if j >= 1:
                            group_root(G_DA + j - 1, 128, T2)
                else:
                    for i in range(24):
                        act.wait_ge(S("tile_done"), b1 + i + 1)
                        if i < 8:
                            nc.scalar.copy(qN[:, i, :], bank[i % 4][:, 0:T]).then_inc(S("pj_ev"), 1)
                        elif i < 16:
                            nc.scalar.copy(kN[:, i - 8, :], bank[i % 4][:, :]).then_inc(S("pj_ev"), 1)
                        else:
                            nc.scalar.copy(vN[:, :, (i - 16) * P:(i - 15) * P],
                                           bank[i % 4][:, :].rearrange("p (a b) -> p a b", a=4)).then_inc(S("pj_ev"), 1)
                        if 1 <= i < 17:
                            j = i - 1
                            act.wait_ge(S("pj_ev"), 32 + i)
                            squares(G_NA + j, [qN[:, j, :] if j < 8 else kN[:, j - 8, :]], T if j < 8 else T2)
                        if 0 <= i - 3 < 16:
                            group_root(G_NA + i - 3, 64, T if i - 3 < 8 else T2)
                        hi(b1 + i + LEAD)
                    for n in range(32, 66):
                        if n < 64:
                            act.wait_ge(S("u_mx"), n + 1)
                            act.wait_ge(S("u_pt"), n - 1)
                            a0 = 24 + 4 * (n % 2)
                            nc.scalar.activation(Pb[n % 2][:, 0, :], Pb[n % 2][:, 1, :], ACT.Exp, bias=col[:, a0:a0 + 1],
                                                 accum_out=col[:, a0 + 2:a0 + 3]).then_inc(S("u_exp"), 1)
                        if 33 <= n <= 64:
                            unit_out(n - 1, 4)
                        if n >= 34:
                            g = n - 2
                            if g % 4 == 3:
                                hc = (g - 32) // 4
                                act.wait_ge(S("u_pv"), g + 1)
                                nc.scalar.copy(mix2[:, hc, XS], bank[6 + hc % 2][:, 0:T]).then_inc(S("o_ev"), 1)
                if l == 0:
                    act.wait_ge(S("gn_out"), G_NA)
                    act.wait_ge(S("u_pv"), 32)
                    split_high("m2", [(Hh[:, c:c + 2, :], mix2[:, c:c + 2, :]) for c in (0, 2, 4, 6)])
                else:
                    act.wait_ge(S("o_ev"), 16)
                    act.wait_ge(S("u_pv"), 64)
                    split_high("m3", [(Hh[:, c:c + 4, XS], mix2[:, c:c + 4, XS]) for c in (0, 4)])
                for m_ in range(C):
                    act.wait_ge(S("tile_done"), b2 + m_ + 1)
                    hi(b2 + m_ + LEAD)
                norm_act(f"f{l}", X[:, :, xs], w_, [(S("res_ev"), 2 * C * l + C)])
                norm_shift(l, f"f{l}", (0, 1) if l == 0 else (1,), 3)
                for m_ in range(KF):
                    act.wait_ge(S("tile_done"), b3 + 2 * m_ + 1)
                    if m_ >= 2:
                        act.wait_ge(S("hid"), KF * l + m_ - 1)
                    nc.scalar.activation(sg[m_ % 2][:, 0:w_], bank[2 * (m_ % 2)][:, 0:w_], ACT.Silu).then_inc(S("silu"), 1)
                    hi(b3 + 2 * m_ + LEAD)
                    act.wait_ge(S("tile_done"), b3 + 2 * m_ + 2)
                    hi(b3 + 2 * m_ + 1 + LEAD)
                b4 = b3 + N_FIN
                act.wait_ge(S("hid"), KF * (l + 1))
                for n in range(KF):
                    act.wait_ge(S("tile_done"), max(b4, b4 + n - MV + 1))
                    j, b = n % (KF // 2), 2 * (n % MV)
                    nc.scalar.copy(Hh[:, b:b + 2, 0:w_], hid[:, 2 * j:2 * j + 2, 0:w_]).then_inc(S("mv_hi"), 1)
                    hi(b4 + n + LEAD)

        @block.vector
        def _(dve):
            v = nc.vector
            order = [0]

            def link(ins):
                order[0] += 1
                ins.then_inc(S("dve_order"), 1)
                return order[0]

            def seq(ins):
                dve.wait_ge(S("dve_order"), link(ins))

            lo_next = [0]

            def lo(upto, it=0):
                while lo_next[0] <= min(upto, (NTILES if stop_after is None else stop_after) - 1):
                    i = lo_next[0]
                    if any(a <= i < b for a, b in POOL_TILES):
                        lo_next[0] += 1
                        continue
                    if any(i == b for _, b in POOL_TILES):
                        dve.wait_ge(S("lo_done"), i)
                    dve.wait_ge(S("hi_done"), i + 1 + R * it)
                    v.tensor_tensor(Wl[:, i % SPL], ring[:, i % RAW], Wh[:, i % SPL], ALU.subtract).then_inc(S("lo_done"), 1)
                    lo_next[0] += 1

            def split_low(name, srcs):
                for n, (o, x_, h_) in enumerate(srcs):
                    dve.wait_ge(S("h_hi"), SPLITS[name][0] + n + 1)
                    v.tensor_tensor(o, x_, h_, ALU.subtract).then_inc(S("h_out"), 1)

            def norm_split(name, x, gains):
                dve.wait_ge(S("norm_rt"), NORMS.index(name) + 1)
                seq(v.reciprocal(rs[:, :], rt[:, :]))
                for c in range(C):
                    m = v.scalar_tensor_tensor(out=sq1[:, c, :], in0=x[:, c, :], scalar=gains[:, c:c + 1],
                                               in1=rs[:, :], op0=ALU.mult, op1=ALU.mult)
                    if c % 4 == 3:
                        m.then_inc(S("h_mul"), 1)
                split_low(name, [(Hl[:, c:c + 4, XS], sq1[:, c:c + 4, :], Hh[:, c:c + 4, XS]) for c in (0, 4)])

            def norm_out(name, x, width, gains, out, shifts=None):
                j = NORMS.index(name)
                dve.wait_ge(S("norm_rt"), j + 1)
                seq(v.reciprocal(rs[:, 0:width], rt[:, 0:width]))
                for c in range(C):
                    m = v.scalar_tensor_tensor(out=out[:, c, :], in0=x[:, c, :], scalar=gains[:, c:c + 1],
                                               in1=rs[:, 0:width], op0=ALU.mult, op1=ALU.mult)
                m.then_inc(S("norm_out"), 1)

            def log1p(u, s1, s2, acc):
                seq(v.tensor_scalar(s1, u, 2.0, None, ALU.add))
                seq(v.reciprocal(s1, s1))
                seq(v.tensor_tensor(s1, u, s1, ALU.mult))
                seq(v.tensor_tensor(s2, s1, s1, ALU.mult))
                seq(v.tensor_scalar(acc, s2, 1.0 / 15, None, ALU.mult))
                for n in (13, 11, 9, 7, 5, 3):
                    seq(v.scalar_tensor_tensor(out=acc, in0=acc, scalar=1.0 / n, in1=s2, op0=ALU.add, op1=ALU.mult))
                seq(v.scalar_tensor_tensor(out=acc, in0=acc, scalar=1.0, in1=s1, op0=ALU.add, op1=ALU.mult))

            v.memset(zero[:, :], 0.0).then_inc(S("setup0"), 1)
            dve.wait_ge(S("setup0"), 1)
            v.memset(eps[:, :], EPS).then_inc(S("setup"), 1)
            dve.wait_ge(S("const_in"), 16)
            lo(LEAD - 1)
            for l in range(L):
                t0 = l * N1
                norm_split(f"n1.{l}", X[:, :, XS], k(f"g1_{l}"))
                z, u, za = fz[0][0:HEADS, :], fz[1][0:HEADS, :], fz[2][0:HEADS, :]
                dve.wait_ge(S("f_mm"), l + 1)
                seq(v.tensor_scalar(z, bank[4][0:HEADS, 0:T], k(f"bf{l}")[0:HEADS, :], None, ALU.add))
                v.scalar_tensor_tensor(out=za, in0=z, scalar=-1.0, in1=z, op0=ALU.mult, op1=ALU.max).then_inc(S("fz_ready"), 1)
                lam = k(f"lam{l}")
                v.scalar_tensor_tensor(out=col[:, 0:2], in0=lam, scalar=-1.0, in1=lam, op0=ALU.mult, op1=ALU.max).then_inc(S("lam_abs"), 1)
                v.memset(ypad[:, :, 0:TAPS - 1], 0.0)
                m = v.memset(rpad[:, :, 0:RTAPS - 1], 0.0)
                m.then_inc(S("pads"), 1)
                seq(v.tensor_copy(sel[0:HEADS, :, :], ident[0:HEADS, 0:HEADS].unsqueeze(2).broadcast_to([HEADS, HEADS, P])))
                lo(t0 + LEAD - 1)
                dve.wait_ge(S("fexp"), l + 1)
                log1p(u, fz[3][0:HEADS, :], fz[4][0:HEADS, :], fz[5][0:HEADS, :])
                seq(v.tensor_scalar(z, z, 0.0, None, ALU.min))
                seq(v.scalar_tensor_tensor(out=z, in0=fz[5][0:HEADS, :], scalar=-2.0, in1=z, op0=ALU.mult, op1=ALU.add))
                seq(v.memset(fz[3][0:HEADS, :], 1.0))
                seq(v.tensor_tensor_scan(cum[0:HEADS, :], fz[3][0:HEADS, :], z, 0.0, ALU.mult, ALU.add))
                v.tensor_scalar(ncum[0:HEADS, :], cum[0:HEADS, :], -1.0, None, ALU.mult).then_inc(S("cum_ready"), 1)
                dve.wait_ge(S("lamexp"), l + 1)
                log1p(col[:, 2:4], col[:, 4:6], col[:, 6:8], col[:, 16:18])
                seq(v.tensor_scalar(col[:, 18:20], lam, -1.0, 0.0, ALU.mult, ALU.max))
                seq(v.scalar_tensor_tensor(out=col[:, 18:20], in0=col[:, 16:18], scalar=2.0, in1=col[:, 18:20],
                                           op0=ALU.mult, op1=ALU.add))
                seq(v.tensor_scalar(col[:, 20:22], col[:, 18:20], -8.0, None, ALU.mult))
                for i in range(4):
                    lo(t0 + i + LEAD)
                dve.wait_ge(S("proj_ev"), N_IN * l + 4)
                seq(v.tensor_tensor(ypad[:, :, TAPS - 1:], cvA[:, :, :], cvG[:, :, :], ALU.mult))
                lo(t0 + 5 + LEAD)
                dve.wait_ge(S("proj_ev"), N_IN * l + 6)

                def conv(out, src, taps, w, b, tile_every=0):
                    last = [0, 0]
                    for j in range(taps):
                        if tile_every and j % tile_every == 1 and lo_next[0] < t0 + N_IN + LEAD:
                            lo(lo_next[0])
                        for c in range(2):
                            if j == 0:
                                last[c] = link(v.tensor_scalar(out[:, c, :], src[:, c, 0:T], w[:, c * taps:c * taps + 1],
                                                               b[:, c:c + 1], ALU.mult, ALU.add))
                            else:
                                dve.wait_ge(S("dve_order"), last[c])
                                last[c] = link(v.scalar_tensor_tensor(
                                    out=out[:, c, :], in0=src[:, c, j:j + T], scalar=w[:, c * taps + j:c * taps + j + 1],
                                    in1=out[:, c, :], op0=ALU.mult, op1=ALU.add))
                    dve.wait_ge(S("dve_order"), last[1])

                conv(xr, rpad, RTAPS, k(f"rw{l}"), k(f"rb{l}"))
                dve.nop().then_inc(S("xr_ready"), 1)
                conv(yconv, ypad, TAPS, k(f"cw{l}"), k(f"cb{l}"), 2)
                dve.nop().then_inc(S("conv_done"), 1)
                dve.wait_ge(S("rg_ev"), 2 * l + 2)
                lo(t0 + N_IN - 1 + LEAD)
                for c in range(2):
                    m = v.tensor_scalar(la[:, c, :], rg[:, c, :], col[:, 20 + c:21 + c], None, ALU.mult)
                m.then_inc(S("loga"), 1)
                seq(v.tensor_tensor(bx[:, :, :], ig[:, :, :], xr[:, :, :], ALU.mult))
                dve.wait_ge(S("rnn_exp"), 2 * l + 2)
                seq(v.tensor_tensor(m2[:, :, :], aa[:, :, :], aa[:, :, :], ALU.mult))
                v.scalar_tensor_tensor(out=m2[:, :, :], in0=m2[:, :, :], scalar=1.0, in1=th[:, :, :],
                                       op0=ALU.add, op1=ALU.mult).then_inc(S("m2_ready"), 1)
                dve.wait_ge(S("rnn_root"), l + 1)
                seq(v.tensor_tensor(bx[:, :, :], bx[:, :, :], m2[:, :, :], ALU.mult))
                for c in range(2):
                    n = link(v.tensor_tensor_scan(hs[:, c, :], aa[:, c, :], bx[:, c, :], 0.0, ALU.mult, ALU.add))
                dve.wait_ge(S("dve_order"), n)
                v.tensor_tensor(mixT[:, 6:8, :], hs[:, :, :], gateG[:, :, :], ALU.mult).then_inc(S("rnn_out"), 1)
                dve.wait_ge(S("bc_mm"), l + 1)
                v.tensor_copy(cT[:, :, :], bank[5][:, 0:2 * HEADS].rearrange("p (a b) -> p a b", a=2))
                for i in range(4):
                    src = bank[(0, 1, 2, 4)[i]][:, :].rearrange("p (a b) -> p a b", a=2)
                    mk = k("mask").unsqueeze(1).broadcast_to([P, 2, P])
                    dst = biasT[:, 2 * i:2 * i + 2, :]
                    v.tensor_tensor(dst[:, :, 0:P], src[:, :, 0:P], mk, ALU.add)
                    v.tensor_copy(dst[:, :, P:2 * P], src[:, :, 0:P])
                    m = v.tensor_tensor(dst[:, :, 2 * P:], src[:, :, P:], mk, ALU.add)
                m.then_inc(S("bc_ev"), 1)
                dve.wait_ge(S("bc_ev"), l + 1)
                for h in range(HEADS + 1):
                    if h < HEADS:
                        dve.wait_ge(S("att_mm"), HEADS * l + h + 1)
                        if h >= 2:
                            dve.wait_ge(S("att_exp"), HEADS * l + h - 1)
                        s_, b = sc[h % 2], bank[4 + h % 2]
                        v.scalar_tensor_tensor(out=s_[:, 0:P], in0=b[:, 0:P], scalar=cT[:, 0, h:h + 1],
                                               in1=biasT[:, h, 0:P], op0=ALU.add, op1=ALU.add)
                        v.scalar_tensor_tensor(out=s_[:, P:], in0=b[:, P:3 * P], scalar=cT[:, 1, h:h + 1],
                                               in1=biasT[:, h, P:], op0=ALU.add, op1=ALU.add).then_inc(S("att_sc"), 1)
                        dve.wait_ge(S("att_sc"), HEADS * l + h + 1)
                        nm = col[:, 8 + 2 * (h % 2):10 + 2 * (h % 2)]
                        v.tensor_reduce(nm[:, 0:1], s_[:, 0:P], AXX, ALU.max, negate=True)
                        v.tensor_reduce(nm[:, 1:2], s_[:, P:], AXX, ALU.max, negate=True).then_inc(S("att_mx"), 1)
                    if h >= 1:
                        g = h - 1
                        dve.wait_ge(S("att_exp"), HEADS * l + g + 1)
                        sm = col[:, 12 + 2 * (g % 2):14 + 2 * (g % 2)]
                        seq(v.reciprocal(sm, sm))
                        v.tensor_scalar(Pm[g % 2][:, 0:P], Pm[g % 2][:, 0:P], sm[:, 0:1], None, ALU.mult)
                        v.tensor_scalar(Pm[g % 2][:, P:], Pm[g % 2][:, P:], sm[:, 1:2], None, ALU.mult)\
                            .then_inc(S("p_ready"), 1)
                dve.wait_ge(S("ln_sum"), l + 1)
                for c in range(2):
                    m = v.scalar_tensor_tensor(out=cen[:, c, :], in0=bank[3][:, 0:T], scalar=-1.0 / 256,
                                               in1=yconv[:, c, :], op0=ALU.mult, op1=ALU.add)
                m.then_inc(S("ln_cen"), 1)
                dve.wait_ge(S("ln_root"), l + 1)
                seq(v.reciprocal(rs[:, 0:T], rt[:, 0:T]))
                for c in range(2):
                    m = v.scalar_tensor_tensor(out=cen[:, c, :], in0=cen[:, c, :], scalar=k(f"lg{l}", c, c + 1),
                                               in1=rs[:, 0:T], op0=ALU.mult, op1=ALU.mult)
                m.then_inc(S("ln_z"), 1)
                split_low(f"m{l}", [(Hl[:, c:c + 4, XS], mixT[:, c:c + 4, :], Hh[:, c:c + 4, XS]) for c in (0, 4)])
                for m_ in range(N_OUT):
                    lo(t0 + N_IN + m_ + LEAD)
                    dve.wait_ge(S("tile_done"), l * N1 + N_IN + m_ + 1)
                    v.tensor_tensor(X[:, m_, XS], X[:, m_, XS], bank[m_ % 4][:, 0:T], ALU.add).then_inc(S("op_ev"), 1)
                norm_split(f"n2.{l}", X[:, :, XS], k(f"g2_{l}"))

                def top16(vals, idx, src, scratch):
                    seq(v.max(vals[:, 0:8], src))
                    v.max_index(idx[:, 0:8], vals[:, 0:8], src)
                    seq(v.match_replace(scratch, vals[:, 0:8], src, -3.0e38))
                    seq(v.max(vals[:, 8:16], scratch))
                    return v.max_index(idx[:, 8:16], vals[:, 8:16], scratch)

                for j in range(N_WQ):
                    lo(t0 + N_IN + N_OUT + j + LEAD)
                    dve.wait_ge(S("s_mm"), N_WQ * l + j + 1)
                    for tt in range(2):
                        n = link(top16(v12[:, tt, j, :], i12u[:, tt, j, :], bank[2 + j % 2][:, tt * P:(tt + 1) * P], w1[:, :]))
                        dve.wait_ge(S("dve_order"), n)
                    dve.nop().then_inc(S("top_ev"), 1)
                seq(v.tensor_copy(if12[:, :, :, :].rearrange("p a b c -> p (a b c)"),
                                  i12u[:, :, :, :].rearrange("p a b c -> p (a b c)")))
                p0 = t0 + N_IN + N_OUT + N_WQ

                def beside():
                    if lo_next[0] < p0 + EQ + LEAD:
                        lo(lo_next[0])

                for tt in range(2):
                    for h in range(PH):
                        beside()
                        seq(v.tensor_tensor(cand[:, :].rearrange("p (a b) -> p a b", a=16),
                                            v12[:, tt, 2 * h, :].unsqueeze(2).broadcast_to([P, 16, 16]),
                                            v12[:, tt, 2 * h + 1, :].unsqueeze(1).broadcast_to([P, 16, 16]), ALU.add))
                        seq(top16(sv[:, tt, h, :], ciu[:, tt, h, :], cand[:, :], cand2[:, :]))
                    cf = ciu[:, tt, :, :].rearrange("p a b -> p (a b)")
                    au = cau[:, tt, :, :].rearrange("p a b -> p (a b)")
                    bu = cbu[:, tt, :, :].rearrange("p a b -> p (a b)")
                    seq(v.tensor_scalar(au, cf, 4, None, ALU.logical_shift_right))
                    seq(v.tensor_scalar(bu, cf, 15, None, ALU.bitwise_and))
                    af = oneh[:, 0, :, :].rearrange("p a b -> p (a b)")
                    seq(v.tensor_copy(af[:, 0:P], au))
                    seq(v.tensor_copy(af[:, P:2 * P], bu))
                    seq(v.tensor_copy(ca[:, tt, :, :].rearrange("p a b -> p (a b)"), af[:, 0:P]))
                    seq(v.tensor_copy(cb[:, tt, :, :].rearrange("p a b -> p (a b)"), af[:, P:2 * P]))
                    for half, rank in ((0, ca), (1, cb)):
                        beside()
                        io = k("iota", 0, 16).unsqueeze(1).unsqueeze(1).broadcast_to([P, 8, 16, 16])
                        seq(v.tensor_tensor(oneh, rank[:, tt, :, :].unsqueeze(3).broadcast_to([P, 8, 16, 16]), io, ALU.is_equal))
                        beside()
                        keys = if12[:, tt, :, :].rearrange("p (h two) s -> p h two s", two=2)[:, :, half, :]
                        seq(v.tensor_tensor(oneh, oneh, keys.unsqueeze(2).broadcast_to([P, 8, 16, 16]), ALU.mult))
                        beside()
                        seq(v.tensor_reduce(gte[:, tt, 1 + half, :].rearrange("p (a b) -> p a b", a=8), oneh, AXX, ALU.add))
                    mx = sv[:, tt, :, 0:1]
                    seq(v.tensor_copy(ssum[:, tt, :].unsqueeze(2), mx))
                    v.tensor_tensor(sv[:, tt, :, :], sv[:, tt, :, :], ssum[:, tt, :].unsqueeze(2).broadcast_to([P, 8, 16]),
                                    ALU.subtract).then_inc(S("sv_sub"), 1)
                lo(p0 + EQ - 1 + LEAD)
                for tt in range(2):
                    dve.wait_ge(S("sv_exp"), 2 * l + tt + 1)
                    g3 = gte[:, tt, 0, :].rearrange("p (a b) -> p a b", a=8)
                    seq(v.tensor_reduce(ssum[:, tt, :], g3, AXX, ALU.add))
                    seq(v.reciprocal(ssum[:, tt, :], ssum[:, tt, :]))
                    v.tensor_tensor(g3, g3, ssum[:, tt, :].unsqueeze(2).broadcast_to([P, 8, 16]), ALU.mult)\
                        .then_inc(S("gate_ready"), 1)
                for tt in range(2):
                    dve.wait_ge(S("gt_mm"), 2 * l + tt + 1)
                    v.tensor_copy(gT[:, :, tt * P:(tt + 1) * P], bank[2 + tt][:, 0:3 * P].rearrange("p (a b) -> p a b", a=3))\
                        .then_inc(S("gt_ev"), 1)
                dve.wait_ge(S("gt_ev"), 2 * (l + 1))
                for pi, (kind, q, qb) in enumerate(PHASES):
                    if pi == 0:
                        continue
                    base = p0 + pi * EQ
                    if qb is not None:
                        dve.wait_ge(S("h_ev"), 2 + NKEY * l + (qb + 1) * EQ)

                    def spread(it, s, qb=qb):
                        n = NKEY * l + qb * EQ + s + R * it
                        after(dve, S("g_mm"), n - 1)
                        io = k("iota", qb * EQ, (qb + 1) * EQ).unsqueeze(1).broadcast_to([P, BT, EQ])
                        at = bass.ds(it * (R * BT) + s * BT, BT)
                        v.tensor_tensor(Aoh[s % 2], gT[:, 1, at].unsqueeze(2).broadcast_to([P, BT, P]),
                                        k("iota").unsqueeze(1).broadcast_to([P, BT, P]), ALU.is_equal)\
                            .then_inc(S("a_ready"), 1)
                        v.tensor_tensor(Boh[s % 2], gT[:, 2, at].unsqueeze(2).broadcast_to([P, BT, EQ]), io,
                                        ALU.is_equal).then_inc(S("b_hot"), 1)
                        dve.wait_ge(S("b_hot"), n + 1)
                        v.tensor_tensor(Bg[s % 2], Boh[s % 2], gT[:, 0, at].unsqueeze(2).broadcast_to([P, BT, EQ]),
                                        ALU.mult).then_inc(S("b_ready"), 1)

                    def gated(it, s, qb=qb):
                        n = NKEY * l + qb * EQ + s + R * it
                        dve.wait_ge(S("g_mm"), n + 1)
                        at = bass.ds(it * (R * BT) + s * BT, BT)
                        g = GH[qb % 2][:, :, at].rearrange("p e t -> p t e")
                        v.tensor_tensor(g, g, bank[2 + s % 2][:, 0:BT * EQ].rearrange("p (t e) -> p t e", t=BT),
                                        ALU.mult).then_inc(S("gm_ev"), 1)

                    def body(it, kind=kind, q=q, qb=qb, base=base):
                        for s in range(R):
                            if kind == "v":
                                dve.wait_ge(S("mv_hi"), NKEY * l + q * EQ + s + 1 + R * it)
                                v.tensor_tensor(Hl[:, s % MV, 0:T], GH[q % 2][:, bass.ds(it * R + s, 1), :]
                                                .rearrange("p o t -> p (o t)"), Hh[:, s % MV, 0:T], ALU.subtract)\
                                    .then_inc(S("mv_lo"), 1)
                            if qb is not None:
                                spread(it, s)
                            lo_next[0] = base + s + LEAD
                            lo(base + s + LEAD, it)
                            if qb is not None and (s or not isinstance(it, int) or it):
                                gated(it, s - 1)

                    steps(dve, EQ // R, qb is not None, body)
                    if qb is not None:
                        gated(EQ // R - 1, R - 1)
                    lo_next[0] = base + EQ + LEAD
                dve.wait_ge(S("acc_done"), l + 1)
                for i in range(4):
                    m = v.tensor_tensor(X[:, 2 * i:2 * i + 2, XS], X[:, 2 * i:2 * i + 2, XS],
                                        bank[4 + i][:, :].rearrange("p (a b) -> p a b", a=2), ALU.add)
                m.then_inc(S("peer_out"), 1)
                dve.wait_ge(S("peer_out"), l + 1)
            norm_out("fin", X[:, :, XS], T, k("gfin"), X[:, :, XS])

            dve.wait_ge(S("norm_out"), 1)
            seq(v.tensor_tensor(col[:, 60:62], k("lq"), k("lk"), ALU.mult))
            dve.nop().then_inc(S("lam_prod"), 1)
            dve.wait_ge(S("lam_exp"), 1)
            seq(v.tensor_tensor(nlam[:, :], col[:, 62:63], col[:, 63:64], ALU.subtract))
            seq(v.tensor_scalar(nlam[:, :], nlam[:, :], LAM_INIT, None, ALU.add))
            for a, name, scale in ((64, "daq", 0.125), (65, "mqn", 192 ** -0.5), (66, "mqr", 192 ** -0.5),
                                   (67, "naq", 0.125), (68, "dao", 1.0 - LAM_INIT)):
                seq(v.tensor_scalar(col[:, a:a + 1], k(name), scale, None, ALU.mult))

            def norm_scaled(l, name, gains, halves, width, sh):
                j = NORMS.index(name)
                dve.wait_ge(S("norm_rt"), j + 1)
                seq(v.reciprocal(rs2[:, 0:width], rt2[:, 0:width]))
                for c in range(C):
                    for s_ in halves:
                        xs = slice(s_ * T, (s_ + 1) * T)
                        rsl = rs2[:, xs] if len(halves) == 2 else rs2[:, 0:T]
                        v.scalar_tensor_tensor(out=sq2[:, c, xs], in0=X[:, c, xs], scalar=gains[:, c, s_:s_ + 1], in1=rsl,
                                               op0=ALU.mult, op1=ALU.mult).then_inc(S("h_mul"), 1)
                n = SPLITS[name][0]
                for c in range(C):
                    for s_ in halves:
                        n += 1
                        xs = slice(s_ * T, (s_ + 1) * T)
                        dve.wait_ge(S("h_hi"), n)
                        v.scalar_tensor_tensor(out=Hl[:, c, xs], in0=sq2[:, c, xs], scalar=modv[l][:, sh * C + c, s_:s_ + 1],
                                               in1=Hh[:, c, xs], op0=ALU.add, op1=ALU.subtract).then_inc(S("h_out"), 1)

            def group_norm(j, tiles_, width, last=True):
                dve.wait_ge(S("gn_rt"), j + 1)
                seq(v.reciprocal(grs[j % 2][:, 0:width], grt[j % 2][:, 0:width]))
                for t_, gain in tiles_:
                    m = v.scalar_tensor_tensor(out=t_, in0=t_, scalar=gain, in1=grs[j % 2][:, 0:width],
                                               op0=ALU.mult, op1=ALU.mult)
                m.then_inc(S("gn_out"), 1)

            def residual(l, m_, b, gate, count):
                for s_ in ((0, 1) if l == 0 else (1,)):
                    xs = slice(s_ * T, (s_ + 1) * T)
                    src = bank[b][:, xs] if l == 0 else bank[b][:, 0:T]
                    m = v.scalar_tensor_tensor(out=X[:, m_, xs], in0=src, scalar=modv[l][:, gate * C + m_, s_:s_ + 1],
                                               in1=X[:, m_, xs], op0=ALU.mult, op1=ALU.add)
                m.then_inc(S("res_ev"), 1)

            for l in range(L):
                b0 = SB[l]
                b1 = b0 + N_MOD
                b2 = b1 + PROJ[l]
                b3 = b2 + N_OUT
                b4 = b3 + N_FIN
                w_ = T2 if l == 0 else T
                if l == 0:
                    dve.wait_ge(S("csil"), 2)
                    v.tensor_tensor(cs[:, 1], csil, cs[:, 0], ALU.subtract).then_inc(S("cs_split"), 1)
                lo(b1 - 1 + LEAD)
                dve.wait_ge(S("tile_done"), b1)
                seq(v.tensor_tensor(modv[l], bank[5][:, 0:2 * N_MOD].rearrange("p (a b) -> p a b", b=2),
                                    k(f"mb{l}").unsqueeze(2).broadcast_to([P, N_MOD, 2]), ALU.add))
                for dst, chunk, gname in ((gA, 1, f"gm{l}"), (gF, 4, f"gf{l}")):
                    seq(v.tensor_scalar(dst, modv[l][:, chunk * C:(chunk + 1) * C, :], 1.0, None, ALU.add))
                    seq(v.tensor_tensor(dst, dst, k(gname).unsqueeze(2).broadcast_to([P, C, 2]), ALU.mult))
                norm_scaled(l, f"a{l}", gA, (0, 1), T2, 0)
                if l == 0:
                    gains = [col[:, 64:65]] * 4 + [k("dak")] * 4
                    for j in range(8):
                        lo(b1 + j + 3 + LEAD)
                        group_norm(j, [(raw[:, j, :], gains[j])], T2)
                    lo(b1 + 11 + LEAD)
                    group_norm(8, [(raw[:, 8 + c, :], k("mqa", c, c + 1)) for c in range(2)], T2)
                    lo(b1 + 12 + LEAD)
                    group_norm(9, [(raw[:, 10, :], k("mkva"))], T2)
                    lo(b1 + 13 + LEAD)
                    group_norm(10, [(raw[:, 11, :], k("mkr"))], T2)
                    lo(b1 + 15 + LEAD)
                    for j in range(4):
                        group_norm(G_MLA + j, [(raw2[:, 2 * j, :], col[:, 65:66]), (raw2[:, 2 * j + 1, :], col[:, 66:67])], T2)
                    for j in range(4):
                        group_norm(G_MLA + 4 + j, [(raw2[:, 8 + j, :], k("mk"))], T2)
                    dve.wait_ge(S("gn_ss"), G_DA)
                    for r_, t_ in enumerate(rope_tiles):
                        dve.wait_ge(S("rope_mm"), r_ + 1)
                        v.tensor_tensor(rtmp[0], bank[r_ % 4][:, 0:T], k("sin"), ALU.mult).then_inc(S("rope_ev"), 1)
                        seq(v.tensor_tensor(rtmp[1], t_[:, XS], k("cos"), ALU.mult))
                        dve.wait_ge(S("rope_ev"), r_ + 1)
                        v.tensor_tensor(t_[:, XS], rtmp[0], rtmp[1], ALU.add).then_inc(S("rope_out"), 1)
                        dve.wait_ge(S("rope_out"), r_ + 1)
                    for n in range(33):
                        if n < 32:
                            hh, qt = n // 4, n % 4
                            nk = 2 * P if qt < 2 else T2
                            dve.wait_ge(S("u_mm"), n + 1)
                            a0 = 24 + 4 * (n % 2)
                            for i in range(2 if hh < 4 else 1):
                                m = v.tensor_reduce(col[:, a0 + i:a0 + i + 1], bank[2 * (n % 2) + i][:, 0:nk], AXX, ALU.max,
                                                    negate=True)
                            m.then_inc(S("u_mx"), 1)
                        if n >= 1:
                            g = n - 1
                            nk = 2 * P if g % 4 < 2 else T2
                            a0 = 26 + 4 * (g % 2)
                            p = Pb[g % 2]
                            dve.wait_ge(S("u_exp"), g + 1)
                            if g < 16:
                                seq(v.reciprocal(col[:, a0:a0 + 2], col[:, a0:a0 + 2]))
                                seq(v.tensor_scalar(col[:, a0 + 1:a0 + 2], col[:, a0 + 1:a0 + 2], nlam[:, :], None, ALU.mult))
                                seq(v.tensor_scalar(p[:, 1, 0:nk], p[:, 1, 0:nk], col[:, a0 + 1:a0 + 2], None, ALU.mult))
                                v.scalar_tensor_tensor(out=p[:, 0, 0:nk], in0=p[:, 0, 0:nk], scalar=col[:, a0:a0 + 1],
                                                       in1=p[:, 1, 0:nk], op0=ALU.mult, op1=ALU.subtract).then_inc(S("u_p"), 1)
                            else:
                                seq(v.reciprocal(col[:, a0:a0 + 1], col[:, a0:a0 + 1]))
                                v.tensor_scalar(p[:, 0, 0:nk], p[:, 0, 0:nk], col[:, a0:a0 + 1], None, ALU.mult)\
                                    .then_inc(S("u_p"), 1)
                    for h in range(4):
                        group_norm(G_DA + h, [(mix2[:, h, :], col[:, 68:69])], T2)
                else:
                    for j in range(8):
                        lo(b1 + j + 3 + LEAD)
                        group_norm(G_NA + j, [(qN[:, j, :], col[:, 67:68])], T)
                    for j in range(8):
                        lo(b1 + 8 + j + 3 + LEAD)
                        group_norm(G_NA + 8 + j, [(kN[:, j, :], k("nak"))], T2)
                    lo(b1 + 23 + LEAD)
                    for n in range(32, 65):
                        if n < 64:
                            h, qt = (n - 32) // 2, n % 2
                            a0 = 24 + 4 * (n % 2)
                            dve.wait_ge(S("u_mm"), n + 1)
                            dve.wait_ge(S(f"bias{h % NB}"), 16 * (h // NB + 1))
                            dve.wait_ge(S("u_exp"), n - 1)
                            p, b = Pb[n % 2], bank[2 * (n % 2)]
                            v.tensor_copy(p[:, 1, 0:T], b[:, 0:T])
                            v.tensor_tensor(p[:, 1, T:], b[:, T:], nab[h % NB][:, qt, :], ALU.add).then_inc(S("u_sc"), 1)
                            dve.wait_ge(S("u_sc"), n - 31)
                            v.tensor_reduce(col[:, a0:a0 + 1], p[:, 1, :], AXX, ALU.max, negate=True).then_inc(S("u_mx"), 1)
                        if n >= 33:
                            g = n - 1
                            a0 = 26 + 4 * (g % 2)
                            dve.wait_ge(S("u_exp"), g + 1)
                            seq(v.reciprocal(col[:, a0:a0 + 1], col[:, a0:a0 + 1]))
                            v.tensor_scalar(Pb[g % 2][:, 0, :], Pb[g % 2][:, 0, :], col[:, a0:a0 + 1], None, ALU.mult)\
                                .then_inc(S("u_p"), 1)
                if l == 0:
                    split_low("m2", [(Hl[:, c:c + 2, :], mix2[:, c:c + 2, :], Hh[:, c:c + 2, :]) for c in (0, 2, 4, 6)])
                else:
                    split_low("m3", [(Hl[:, c:c + 4, XS], mix2[:, c:c + 4, XS], Hh[:, c:c + 4, XS]) for c in (0, 4)])
                for m_ in range(C):
                    lo(b2 + m_ + LEAD)
                    dve.wait_ge(S("tile_done"), b2 + m_ + 1)
                    residual(l, m_, m_ % 4, 2, m_)
                dve.wait_ge(S("res_ev"), 2 * C * l + C)
                norm_scaled(l, f"f{l}", gF, (0, 1) if l == 0 else (1,), w_, 3)
                for m_ in range(KF):
                    lo(b3 + 2 * m_ + 1 + LEAD)
                    dve.wait_ge(S("tile_done"), b3 + 2 * m_ + 2)
                    dve.wait_ge(S("silu"), KF * l + m_ + 1)
                    v.tensor_tensor(hid[:, m_, 0:w_], sg[m_ % 2][:, 0:w_], bank[2 * (m_ % 2) + 1][:, 0:w_], ALU.mult)\
                        .then_inc(S("hid"), 1)
                for half in range(2):
                    for j in range(KF // 2):
                        n = half * (KF // 2) + j
                        b = 2 * (n % MV)
                        dve.wait_ge(S("mv_hi"), L * NKEY + KF * l + n + 1)
                        v.tensor_tensor(Hl[:, b:b + 2, 0:w_], hid[:, 2 * j:2 * j + 2, 0:w_], Hh[:, b:b + 2, 0:w_], ALU.subtract)\
                            .then_inc(S("mv_lo"), 1)
                        lo(b4 + n + LEAD)
                    dve.wait_ge(S("tile_done"), b4 + (half + 1) * (KF // 2))
                    for m_ in range(4):
                        residual(l, 4 * half + m_, 4 * (1 - half) + m_, 5, m_)
                dve.wait_ge(S("res_ev"), 2 * C * (l + 1))

        @block.gpsimd
        def _(pool):
            def rests(n):
                a, b = POOL_TILES[n]
                pool.wait_ge(S("lo_done"), a)

                def body(it):
                    for s in range(R):
                        i = a + s
                        pool.wait_ge(S("hi_done"), i + 1 + R * it)
                        nc.gpsimd.tensor_tensor(Wl[:, i % SPL], ring[:, i % RAW], Wh[:, i % SPL], ALU.subtract)\
                            .then_inc(S("lo_done"), 1)
                steps(pool, (b - a) // R, False, body)

            pool.wait_ge(S("const_in"), 16)
            for l in range(L):
                pool.wait_ge(S("h_out"), SPLITS[f"m{l}"][1])
                pool.dma_start(keysT.rearrange("p a b -> p (a b)"), keys_d[l]).then_inc(S("keys_in"), 16)
                rests(l)
            rests(L)
            pool.wait_ge(S("tile_done"), SB[0] + N_MOD + PROJ[0])
            pool.dma_start(mlaw.rearrange("p a b -> p (a b)"), mla_d).then_inc(S("mla_in"), 16)
            rests(L + 1)
            for h in range(16):
                if h >= NB:
                    pool.wait_ge(S("u_sc"), 2 * (h - NB + 1))
                pool.dma_start(nab[h % NB].rearrange("p a b -> p (a b)"), bias_d[h]).then_inc(S(f"bias{h % NB}"), 16)


def kernel(**inputs):
    import concourse.bacc as _bacc
    from concourse.bass_utils import run_bass_kernel_spmd as _run

    i = {n: np.asarray(a) for n, a in inputs.items()}
    arrays = {
        "weights": weight_stream(i), "constants": constants(i), "keys": key_blocks(i), "mla": mla_blocks(i),
        "bias": na_bias(i), "x": np.ascontiguousarray(i["x"][0].T), "context": np.ascontiguousarray(i["ctx_2"][0].T),
    }
    nc = _bacc.Bacc("TRN2", target_bir_lowering=False, num_devices=1)
    aps = {n: nc.dram_tensor(n, a.shape, F32, kind="ExternalInput").ap() for n, a in arrays.items()}
    out = nc.dram_tensor("out", (D, T), F32, kind="ExternalOutput").ap()
    build(nc, aps["weights"], aps["constants"], aps["keys"], aps["mla"], aps["bias"], aps["x"], aps["context"], out)
    r = _run(nc, [arrays], core_ids=[0])
    return np.ascontiguousarray(r.results[0]["out"].T)[None]
```
